# Optimizing a Trainium2 kernel written in Bass

```python
import math
import jax
import jax.numpy as jnp
from jax import lax
import numpy as np

D_MODEL = 1024
BATCH = 1
SEQ = 512
DEPTH = 2

N_MIXERS = 4
F32 = jnp.float32
ROPE_THETA = 10000.0
DEEPNORM_ALPHA = (2.0 * DEPTH) ** 0.25
DEEPNORM_BETA = (8.0 * DEPTH) ** -0.25
LN_EPS = 1e-5
NEG_INF = -1e30
D_FF = ((8 * D_MODEL + 3 * 256 - 1) // (3 * 256)) * 256

RWKV_HEAD_DIM = 64
RWKV_HEADS = D_MODEL // RWKV_HEAD_DIM
RWKV_LORA_DECAY = 64
RWKV_LORA_ICLR = 64
RWKV_LORA_GATE = 128
RWKV_GN_EPS = 64e-5
GDN_HEAD_DIM = 128
GDN_HEADS = D_MODEL // GDN_HEAD_DIM
GDN_CONV = 4
GDN_CHUNK = 64
GDN_QKV = 3 * GDN_HEADS * GDN_HEAD_DIM
GDN_PROJ = 4 * GDN_HEADS * GDN_HEAD_DIM + 2 * GDN_HEADS
DIFF_HEADS = 8
DIFF_HEAD_DIM = D_MODEL // (2 * DIFF_HEADS)
ATTN_Q_BLOCK = 128
SWA_HEAD_DIM = 64
SWA_Q_HEADS = D_MODEL // SWA_HEAD_DIM
SWA_KV_HEADS = SWA_Q_HEADS // 8
SWA_WINDOW = 128
SWA_QKV = (SWA_Q_HEADS + 2 * SWA_KV_HEADS) * SWA_HEAD_DIM


def _layer_norm(x, g, b):
    xf = x.astype(F32)
    mu = jnp.mean(xf, -1, keepdims=True)
    var = jnp.mean(jnp.square(xf - mu), -1, keepdims=True)
    return ((xf - mu) * lax.rsqrt(var + LN_EPS) * g + b).astype(x.dtype)

def _rms_norm(x, g, eps):
    xf = x.astype(F32)
    return xf * lax.rsqrt(jnp.mean(xf * xf, -1, keepdims=True) + eps) * g

def _l2norm(x, eps=1e-6):
    xf = x.astype(F32)
    return (xf * lax.rsqrt(jnp.sum(xf * xf, -1, keepdims=True) + eps)).astype(x.dtype)

def _rope(x, pos):
    d = x.shape[-1]
    inv = ROPE_THETA ** (-jnp.arange(0, d, 2, dtype=F32) / d)
    ang = pos.astype(F32)[:, None] * inv[None, :]
    cos = jnp.cos(ang)[None, :, None, :]
    sin = jnp.sin(ang)[None, :, None, :]
    x1, x2 = jnp.split(x.astype(F32), 2, axis=-1)
    return jnp.concatenate([x1 * cos - x2 * sin, x2 * cos + x1 * sin], -1).astype(x.dtype)

def _token_shift(x):
    return jnp.pad(x, ((0, 0), (1, 0), (0, 0)))[:, :-1]

def _causal_depthwise_conv(x, w):
    K, C = w.shape
    return lax.conv_general_dilated(x, w[:, None, :].astype(x.dtype), window_strides=(1,),
                                    padding=[(K - 1, 0)], dimension_numbers=('NWC', 'WIO', 'NWC'),
                                    feature_group_count=C)

def _rwkv7_mixer(u, mu, w_rkv, w0, w1, w2, a0, a1, a2, g1, g2, k_k, k_a, r_k, gn_g, gn_b, w_out):
    B, T, D = u.shape
    H, N = RWKV_HEADS, RWKV_HEAD_DIM
    xx = _token_shift(u) - u
    lerp = lambda i: u + xx * mu[i]
    r = lerp(0) @ w_rkv[0]
    k = lerp(1) @ w_rkv[1]
    v = lerp(2) @ w_rkv[2]
    w_log = -jax.nn.softplus(-(w0 + jnp.tanh(lerp(3) @ w1) @ w2)) - 0.5
    a = jax.nn.sigmoid(a0 + (lerp(4) @ a1) @ a2)
    g = jax.nn.sigmoid(lerp(5) @ g1) @ g2
    heads = lambda t: t.reshape(B, T, H, N)
    kk = _l2norm(heads(k * k_k))
    k = k * (1 + (a - 1) * k_a)
    r, k, v, a = heads(r), heads(k), heads(v), heads(a)
    decay = jnp.exp(-jnp.exp(heads(w_log).astype(F32)))
    tm = lambda t: jnp.moveaxis(t.astype(F32), 1, 0)

    def step(S, inp):
        r_t, k_t, v_t, w_t, a_t, b_t = inp
        sa = jnp.einsum('bhvk,bhk->bhv', S, a_t)
        S = S * w_t[:, :, None, :] + sa[..., None] * b_t[:, :, None, :] + v_t[..., None] * k_t[:, :, None, :]
        return S, jnp.einsum('bhvk,bhk->bhv', S, r_t)

    S0 = jnp.zeros((B, H, N, N), F32)
    _, y = lax.scan(step, S0, (tm(r), tm(k), tm(v), jnp.moveaxis(decay, 1, 0), tm(-kk), tm(kk * a)))
    y = jnp.moveaxis(y, 0, 1)
    mean = jnp.mean(y, -1, keepdims=True)
    var = jnp.mean(jnp.square(y - mean), -1, keepdims=True)
    y = ((y - mean) * lax.rsqrt(var + RWKV_GN_EPS)).reshape(B, T, D) * gn_g + gn_b
    bonus = jnp.sum((r * k * r_k).astype(F32), -1, keepdims=True) * v.astype(F32)
    y = (y + bonus.reshape(B, T, D)).astype(u.dtype)
    return (y * g) @ w_out

def _chunk_gated_delta_rule(q, k, v, g, beta):
    B, T, H, dk = q.shape
    dv = v.shape[-1]
    C = GDN_CHUNK
    n = T // C
    chunks = lambda t: jnp.moveaxis(t.astype(F32).reshape(B, n, C, H, -1), 3, 1)
    q, k, v = chunks(q), chunks(k), chunks(v)
    beta = chunks(beta[..., None])
    gc = jnp.cumsum(chunks(g[..., None])[..., 0], axis=-1)
    k_beta, v_beta = k * beta, v * beta
    idx = jnp.arange(C)
    causal = idx[:, None] >= idx[None, :]
    strict = idx[:, None] > idx[None, :]
    decay = jnp.exp(jnp.where(causal, gc[..., :, None] - gc[..., None, :], -jnp.inf))
    L = jnp.where(strict, jnp.einsum('bhnid,bhnjd->bhnij', k_beta, k) * decay, 0.0)
    eye = jnp.eye(C, dtype=F32)
    tinv = lax.linalg.triangular_solve(eye + L, jnp.broadcast_to(eye, L.shape), left_side=True, lower=True)
    u_c = tinv @ v_beta
    w_c = tinv @ (k_beta * jnp.exp(gc)[..., None])
    a_intra = jnp.where(causal, jnp.einsum('bhnid,bhnjd->bhnij', q, k) * decay, 0.0)
    q_dec = q * jnp.exp(gc)[..., None]
    k_dec = k * jnp.exp(gc[..., -1:] - gc)[..., None]
    g_last = jnp.exp(gc[..., -1])

    def step(S, inp):
        q_i, k_i, u_i, w_i, a_i, gl = inp
        v_new = u_i - w_i @ S
        o = q_i @ S + a_i @ v_new
        S = S * gl[..., None, None] + jnp.einsum('bhck,bhcv->bhkv', k_i, v_new)
        return S, o

    xs = tuple(jnp.moveaxis(t, 2, 0) for t in (q_dec, k_dec, u_c, w_c, a_intra, g_last))
    _, o = lax.scan(step, jnp.zeros((B, H, dk, dv), F32), xs)
    return jnp.transpose(o, (1, 0, 3, 2, 4)).reshape(B, T, H, dv)

def _gated_deltanet_mixer(u, w_in, conv_w, a_log, dt_bias, norm_g, w_out):
    B, T, _ = u.shape
    H, d = GDN_HEADS, GDN_HEAD_DIM
    hd = H * d
    proj = u @ w_in
    qkv = jax.nn.silu(_causal_depthwise_conv(proj[..., :3 * hd], conv_w))
    z = proj[..., 3 * hd:4 * hd].reshape(B, T, H, d)
    b_in = proj[..., 4 * hd:4 * hd + H]
    a_in = proj[..., 4 * hd + H:]
    q = _l2norm(qkv[..., :hd].reshape(B, T, H, d)) * d ** -0.5
    k = _l2norm(qkv[..., hd:2 * hd].reshape(B, T, H, d))
    v = qkv[..., 2 * hd:].reshape(B, T, H, d)
    beta = jax.nn.sigmoid(b_in.astype(F32))
    g = -jnp.exp(a_log.astype(F32)) * jax.nn.softplus(a_in.astype(F32) + dt_bias)
    o = _chunk_gated_delta_rule(q, k, v, g, beta)
    o = _rms_norm(o, norm_g, 1e-6) * jax.nn.silu(z.astype(F32))
    return o.reshape(B, T, hd).astype(u.dtype) @ w_out

def _diff_attention_mixer(u, pos, w_in, lam_p, subln_g, w_out, lam_init):
    B, T, D = u.shape
    H, d, Qb = DIFF_HEADS, DIFF_HEAD_DIM, ATTN_Q_BLOCK
    proj = u @ w_in
    q = _rope(proj[..., :D].reshape(B, T, 2 * H, d), pos) * d ** -0.5
    k = _rope(proj[..., D:2 * D].reshape(B, T, 2 * H, d), pos)
    v = proj[..., 2 * D:].reshape(B, T, H, 2 * d)
    lp = lam_p.astype(F32)
    lam = jnp.exp(jnp.sum(lp[0] * lp[1])) - jnp.exp(jnp.sum(lp[2] * lp[3])) + lam_init
    nb = T // Qb
    qb = jnp.moveaxis(q.reshape(B, nb, Qb, 2 * H, d), 1, 0)
    kf, vf = k.astype(F32), v.astype(F32)
    kpos = jnp.arange(T)

    def block(args):
        q_blk, i = args
        s = jnp.einsum('bqhd,bkhd->bhqk', q_blk.astype(F32), kf)
        qpos = i * Qb + jnp.arange(Qb)
        s = jnp.where(kpos[None, :] <= qpos[:, None], s, NEG_INF)
        p = jax.nn.softmax(s, axis=-1).reshape(B, H, 2, Qb, T)
        attn = p[:, :, 0] - lam * p[:, :, 1]
        return jnp.einsum('bhqk,bkhe->bqhe', attn, vf)

    o = lax.map(block, (qb, jnp.arange(nb)))
    o = jnp.moveaxis(o, 0, 1).reshape(B, T, H, 2 * d)
    o = _rms_norm(o, subln_g, 1e-5) * (1.0 - lam_init)
    return o.reshape(B, T, D).astype(u.dtype) @ w_out

def _swa_sink_mixer(u, pos, w_qkv, b_qkv, sinks, w_out, b_out):
    B, T, _ = u.shape
    Hq, Hkv, d, W = SWA_Q_HEADS, SWA_KV_HEADS, SWA_HEAD_DIM, SWA_WINDOW
    G = Hq // Hkv
    nb = T // W
    proj = u @ w_qkv + b_qkv
    q = _rope(proj[..., :Hq * d].reshape(B, T, Hq, d), pos) * d ** -0.5
    k = _rope(proj[..., Hq * d:(Hq + Hkv) * d].reshape(B, T, Hkv, d), pos)
    v = proj[..., (Hq + Hkv) * d:].reshape(B, T, Hkv, d)
    qb = q.astype(F32).reshape(B, nb, W, Hkv, G, d)

    def band(t):
        tb = t.astype(F32).reshape(B, nb, W, Hkv, d)
        prev = jnp.pad(tb, ((0, 0), (1, 0), (0, 0), (0, 0), (0, 0)))[:, :-1]
        return jnp.concatenate([prev, tb], axis=2)

    kb, vb = band(k), band(v)
    s = jnp.einsum('bnqhgd,bnkhd->bnhgqk', qb, kb)
    qi = jnp.arange(W)[:, None]
    kj = jnp.arange(2 * W)[None, :]
    rel = W + qi - kj
    in_window = (rel >= 0) & (rel < W)
    key_pos = jnp.arange(nb)[:, None] * W + jnp.arange(2 * W)[None, :] - W
    valid = in_window[None, :, :] & (key_pos >= 0)[:, None, :]
    s = jnp.where(valid[None, :, None, None], s, NEG_INF)
    sink = sinks.astype(F32).reshape(Hkv, G)[None, None, :, :, None, None]
    m = jnp.maximum(jnp.max(s, -1, keepdims=True), sink)
    p = jnp.exp(s - m)
    p = p / (jnp.sum(p, -1, keepdims=True) + jnp.exp(sink - m))
    o = jnp.einsum('bnhgqk,bnkhd->bnqhgd', p, vb).reshape(B, T, Hq * d)
    return o.astype(u.dtype) @ w_out + b_out

def _count(m):
    return len(range(m, DEPTH, N_MIXERS))

def first_inputs(seed: int = 0) -> dict:
    key = jax.random.key(seed)
    keys = iter(jax.random.split(key, 48))

    def nrm(shape, std):
        return jax.random.normal(next(keys), shape, F32) * std

    def unif(shape, lo, hi):
        return jax.random.uniform(next(keys), shape, F32, lo, hi)

    D = D_MODEL
    nA, nB, nC, nD = (_count(m) for m in range(N_MIXERS))
    beta = DEEPNORM_BETA
    gdn_hd = GDN_HEADS * GDN_HEAD_DIM
    swa_hd = SWA_Q_HEADS * SWA_HEAD_DIM
    dt = jnp.exp(unif((nB, GDN_HEADS), math.log(1e-3), math.log(1e-1)))
    return {
        'x': nrm((BATCH, SEQ, D), 1.0),
        'c': nrm((BATCH, D), 1.0),
        'ada_w': nrm((DEPTH, D, 6 * D), 0.1 * D ** -0.5),
        'ada_b': nrm((DEPTH, 6 * D), 0.02),
        'ln_g': 1.0 + nrm((DEPTH, 2, D), 0.02),
        'ln_b': nrm((DEPTH, 2, D), 0.02),
        'ffn_w_in': nrm((DEPTH, D, 2 * D_FF), D ** -0.5),
        'ffn_w_out': nrm((DEPTH, D_FF, D), beta * D_FF ** -0.5),
        'rwkv_mu': unif((nA, 6, D), 0.0, 1.0),
        'rwkv_w_rkv': nrm((nA, 3, D, D), D ** -0.5),
        'rwkv_w0': unif((nA, D), -6.0, 1.0),
        'rwkv_w1': nrm((nA, D, RWKV_LORA_DECAY), D ** -0.5),
        'rwkv_w2': nrm((nA, RWKV_LORA_DECAY, D), 0.5 * RWKV_LORA_DECAY ** -0.5),
        'rwkv_a0': nrm((nA, D), 0.1),
        'rwkv_a1': nrm((nA, D, RWKV_LORA_ICLR), D ** -0.5),
        'rwkv_a2': nrm((nA, RWKV_LORA_ICLR, D), 0.5 * RWKV_LORA_ICLR ** -0.5),
        'rwkv_g1': nrm((nA, D, RWKV_LORA_GATE), D ** -0.5),
        'rwkv_g2': nrm((nA, RWKV_LORA_GATE, D), RWKV_LORA_GATE ** -0.5),
        'rwkv_k_k': 1.0 + nrm((nA, D), 0.1),
        'rwkv_k_a': 1.0 + nrm((nA, D), 0.1),
        'rwkv_r_k': nrm((nA, RWKV_HEADS, RWKV_HEAD_DIM), 0.1),
        'rwkv_gn_g': 1.0 + nrm((nA, D), 0.02),
        'rwkv_gn_b': nrm((nA, D), 0.02),
        'rwkv_w_out': nrm((nA, D, D), beta * D ** -0.5),
        'gdn_w_in': nrm((nB, D, GDN_PROJ), D ** -0.5),
        'gdn_conv': nrm((nB, GDN_CONV, GDN_QKV), GDN_CONV ** -0.5),
        'gdn_a_log': jnp.log(unif((nB, GDN_HEADS), 1.0, 16.0)),
        'gdn_dt_bias': dt + jnp.log(-jnp.expm1(-dt)),
        'gdn_norm_g': 1.0 + nrm((nB, GDN_HEAD_DIM), 0.02),
        'gdn_w_out': nrm((nB, gdn_hd, D), beta * gdn_hd ** -0.5),
        'diff_w_in': nrm((nC, D, 3 * D), D ** -0.5),
        'diff_lambda': nrm((nC, 4, DIFF_HEAD_DIM), 0.1),
        'diff_subln_g': 1.0 + nrm((nC, 2 * DIFF_HEAD_DIM), 0.02),
        'diff_w_out': nrm((nC, D, D), beta * D ** -0.5),
        'swa_w_qkv': nrm((nD, D, SWA_QKV), D ** -0.5),
        'swa_b_qkv': nrm((nD, SWA_QKV), 0.02),
        'swa_sinks': nrm((nD, SWA_Q_HEADS), 1.0),
        'swa_w_out': nrm((nD, swa_hd, D), beta * swa_hd ** -0.5),
        'swa_b_out': nrm((nD, D), 0.02),
    }

def first_block(x, c, ada_w, ada_b, ln_g, ln_b, ffn_w_in, ffn_w_out,
              rwkv_mu, rwkv_w_rkv, rwkv_w0, rwkv_w1, rwkv_w2, rwkv_a0, rwkv_a1, rwkv_a2,
              rwkv_g1, rwkv_g2, rwkv_k_k, rwkv_k_a, rwkv_r_k, rwkv_gn_g, rwkv_gn_b, rwkv_w_out,
              gdn_w_in, gdn_conv, gdn_a_log, gdn_dt_bias, gdn_norm_g, gdn_w_out,
              diff_w_in, diff_lambda, diff_subln_g, diff_w_out,
              swa_w_qkv, swa_b_qkv, swa_sinks, swa_w_out, swa_b_out):
    T = x.shape[1]
    pos = jnp.arange(T)
    cond = jax.nn.silu(c)
    for i in range(DEPTH):
        mod = (cond @ ada_w[i] + ada_b[i])[:, None, :]
        sh1, sc1, ga1, sh2, sc2, ga2 = jnp.split(mod, 6, axis=-1)
        u = x * (1 + sc1) + sh1
        m, j = i % N_MIXERS, i // N_MIXERS
        if m == 0:
            y = _rwkv7_mixer(u, rwkv_mu[j], rwkv_w_rkv[j], rwkv_w0[j], rwkv_w1[j], rwkv_w2[j],
                             rwkv_a0[j], rwkv_a1[j], rwkv_a2[j], rwkv_g1[j], rwkv_g2[j],
                             rwkv_k_k[j], rwkv_k_a[j], rwkv_r_k[j], rwkv_gn_g[j], rwkv_gn_b[j],
                             rwkv_w_out[j])
        elif m == 1:
            y = _gated_deltanet_mixer(u, gdn_w_in[j], gdn_conv[j], gdn_a_log[j], gdn_dt_bias[j],
                                      gdn_norm_g[j], gdn_w_out[j])
        elif m == 2:
            lam_init = 0.8 - 0.6 * math.exp(-0.3 * i)
            y = _diff_attention_mixer(u, pos, diff_w_in[j], diff_lambda[j], diff_subln_g[j],
                                      diff_w_out[j], lam_init)
        else:
            y = _swa_sink_mixer(u, pos, swa_w_qkv[j], swa_b_qkv[j], swa_sinks[j], swa_w_out[j],
                                swa_b_out[j])
        x = _layer_norm(DEEPNORM_ALPHA * x + (1 + ga1) * y, ln_g[i, 0], ln_b[i, 0])
        u = x * (1 + sc2) + sh2
        gate, up = jnp.split(u @ ffn_w_in[i], 2, axis=-1)
        y = (jax.nn.silu(gate) * up) @ ffn_w_out[i]
        x = _layer_norm(DEEPNORM_ALPHA * x + (1 + ga2) * y, ln_g[i, 1], ln_b[i, 1])
    return x


N_MIXERS_2 = 2

SSD_D_INNER = 2 * D_MODEL
SSD_HEAD_DIM = 64
SSD_N_HEADS = SSD_D_INNER // SSD_HEAD_DIM
SSD_N_GROUPS = 4
SSD_HEADS_PER_GROUP = SSD_N_HEADS // SSD_N_GROUPS
SSD_D_STATE = 128
SSD_D_CONV = 4
SSD_CHUNK = 128
SSD_CONV_DIM = SSD_D_INNER + 2 * SSD_N_GROUPS * SSD_D_STATE
SSD_D_IN_PROJ = SSD_D_INNER + SSD_CONV_DIM + SSD_N_HEADS

ATT_HEAD_DIM = 64
ATT_HEADS_PER_GROUP = 8
ATT_PATTERNS = ((128, 1), (512, 4), (2048, 16))
ATT_N_GROUPS = len(ATT_PATTERNS)
ATT_QKV_DIM = ATT_N_GROUPS * 3 * ATT_HEADS_PER_GROUP * ATT_HEAD_DIM
ATT_OUT_DIM = ATT_HEADS_PER_GROUP * ATT_HEAD_DIM
ROPE_THETA_2 = 500000.0
ROPE_DIM = ATT_HEAD_DIM // 4

MOE_N_GROUPS = 4
MOE_EXPERTS_PER_GROUP = 8
MOE_N_EXPERTS = MOE_N_GROUPS * MOE_EXPERTS_PER_GROUP
MOE_TOP_K = 2
MOE_HIDDEN = 512
MOE_BLOCK = 128

DEEPNORM_ALPHA_2 = (2 * DEPTH) ** 0.25
DEEPNORM_BETA_2 = (8 * DEPTH) ** -0.25
RMS_EPS = 1e-5
NEG_INF_2 = -1e30


def _layer_norm_2(x, g, b):
    xf = x.astype(jnp.float32)
    mu = jnp.mean(xf, -1, keepdims=True)
    var = jnp.mean(jnp.square(xf - mu), -1, keepdims=True)
    return ((xf - mu) * lax.rsqrt(var + LN_EPS) * g + b).astype(x.dtype)

def _rope_tables(positions):
    inv_freq = ROPE_THETA_2 ** (-jnp.arange(0, ROPE_DIM, 2, dtype=jnp.float32) / ROPE_DIM)
    ang = positions.astype(jnp.float32)[..., None] * inv_freq
    return jnp.cos(ang)[:, :, None, :], jnp.sin(ang)[:, :, None, :]

def _apply_partial_rope(t, cos, sin):
    half = ROPE_DIM // 2
    t1, t2, rest = t[..., :half], t[..., half:ROPE_DIM], t[..., ROPE_DIM:]
    cos = cos.astype(t.dtype)
    sin = sin.astype(t.dtype)
    return jnp.concatenate([t1 * cos - t2 * sin, t2 * cos + t1 * sin, rest], -1)

def _causal_depthwise_conv_2(u, w, b):
    c = u.shape[-1]
    y = lax.conv_general_dilated(u, w.reshape(SSD_D_CONV, 1, c), window_strides=(1,),
                                 padding=((SSD_D_CONV - 1, 0),),
                                 dimension_numbers=('NWC', 'WIO', 'NWC'),
                                 feature_group_count=c)
    return y + b

def _ssd_chunked_scan(x, dt, a, b_in, c_in):
    bsz, s = x.shape[:2]
    nc = s // SSD_CHUNK
    Q, G, E, P, N = SSD_CHUNK, SSD_N_GROUPS, SSD_HEADS_PER_GROUP, SSD_HEAD_DIM, SSD_D_STATE
    xr = (x.astype(jnp.float32) * dt[..., None]).reshape(bsz, nc, Q, G, E, P)
    da = (dt * a).reshape(bsz, nc, Q, G, E).transpose(0, 1, 3, 4, 2)
    br = b_in.astype(jnp.float32).reshape(bsz, nc, Q, G, N)
    cr = c_in.astype(jnp.float32).reshape(bsz, nc, Q, G, N)
    da_cs = jnp.cumsum(da, -1)
    causal = jnp.tril(jnp.ones((Q, Q), bool))
    decay_in = jnp.exp(jnp.where(causal, da_cs[..., :, None] - da_cs[..., None, :], -jnp.inf))
    cb = jnp.einsum('bclgn,bcsgn->bcgls', cr, br)
    y_diag = jnp.einsum('bcgls,bcgels,bcsgep->bclgep', cb, decay_in, xr)
    decay_to_end = jnp.exp(da_cs[..., -1:] - da_cs)
    states = jnp.einsum('bclgn,bcgel,bclgep->bcgepn', br, decay_to_end, xr)
    chunk_decay = jnp.exp(da_cs[..., -1])

    def step(h, inp):
        s_c, dec_c = inp
        return h * dec_c[..., None, None] + s_c, h

    h0 = jnp.zeros((bsz, G, E, P, N), jnp.float32)
    _, prev = lax.scan(step, h0, (jnp.moveaxis(states, 1, 0), jnp.moveaxis(chunk_decay, 1, 0)))
    prev = jnp.moveaxis(prev, 0, 1)
    y_off = jnp.einsum('bclgn,bcgepn,bcgel->bclgep', cr, prev, jnp.exp(da_cs))
    return (y_diag + y_off).reshape(bsz, s, G * E, P)

def _ssd_mixer(x, w_in, conv_w, conv_b, dt_bias, a_log, d_skip, norm_w, w_out):
    bsz, s, _ = x.shape
    zxbcdt = x @ w_in
    z = zxbcdt[..., :SSD_D_INNER]
    xbc = zxbcdt[..., SSD_D_INNER:SSD_D_INNER + SSD_CONV_DIM]
    dt_raw = zxbcdt[..., SSD_D_INNER + SSD_CONV_DIM:]
    xbc = jax.nn.silu(_causal_depthwise_conv_2(xbc, conv_w, conv_b))
    gn = SSD_N_GROUPS * SSD_D_STATE
    xs = xbc[..., :SSD_D_INNER].reshape(bsz, s, SSD_N_HEADS, SSD_HEAD_DIM)
    b_in = xbc[..., SSD_D_INNER:SSD_D_INNER + gn].reshape(bsz, s, SSD_N_GROUPS, SSD_D_STATE)
    c_in = xbc[..., SSD_D_INNER + gn:].reshape(bsz, s, SSD_N_GROUPS, SSD_D_STATE)
    dt = jax.nn.softplus((dt_raw + dt_bias).astype(jnp.float32))
    a = -jnp.exp(a_log.astype(jnp.float32))
    y = _ssd_chunked_scan(xs, dt, a, b_in, c_in) + xs.astype(jnp.float32) * d_skip.astype(jnp.float32)[:, None]
    y = y.reshape(bsz, s, SSD_D_INNER) * jax.nn.silu(z.astype(jnp.float32))
    yg = y.reshape(bsz, s, SSD_N_GROUPS, -1)
    yg = yg * lax.rsqrt(jnp.mean(jnp.square(yg), -1, keepdims=True) + RMS_EPS)
    y = (yg.reshape(bsz, s, SSD_D_INNER) * norm_w).astype(x.dtype)
    return y @ w_out

def _dilated_window_attention(q, k, v, window, dilation):
    bsz, s, h, d = q.shape
    w = window // dilation
    n = s // dilation
    nb = -(-n // w)
    n_pad = nb * w - n

    def to_residues(t):
        return t.reshape(bsz, n, dilation, h, d).transpose(0, 2, 1, 3, 4)

    def key_blocks(t):
        t = jnp.pad(to_residues(t), ((0, 0), (0, 0), (w, n_pad), (0, 0), (0, 0)))
        t = t.reshape(bsz, dilation, nb + 1, w, h, d)
        return jnp.concatenate([t[:, :, :-1], t[:, :, 1:]], axis=3)

    q_r = jnp.pad(to_residues(q), ((0, 0), (0, 0), (0, n_pad), (0, 0), (0, 0)))
    q_r = q_r.reshape(bsz, dilation, nb, w, h, d).astype(jnp.float32)
    k_b = key_blocks(k).astype(jnp.float32)
    v_b = key_blocks(v).astype(jnp.float32)
    scores = jnp.einsum('brnqhd,brnkhd->brnhqk', q_r, k_b) * (ATT_HEAD_DIM ** -0.5)
    qi = jnp.arange(w)[:, None]
    ki = jnp.arange(2 * w)[None, :]
    blk = jnp.arange(nb)[:, None, None]
    valid = (ki >= qi) & (ki <= qi + w) & (blk * w + ki - w >= 0)
    scores = jnp.where(valid[None, None, :, None], scores, NEG_INF_2)
    m = jnp.max(scores, -1)
    p = jnp.exp(scores - m[..., None])
    l = jnp.sum(p, -1)
    m_t = m.transpose(0, 1, 2, 4, 3)
    l_t = l.transpose(0, 1, 2, 4, 3)
    o = jnp.einsum('brnhqk,brnkhd->brnqhd', p, v_b) / l_t[..., None]

    def from_residues(t):
        t = t.reshape(bsz, dilation, nb * w, *t.shape[4:])[:, :, :n]
        t = jnp.moveaxis(t, 1, 2)
        return t.reshape(bsz, s, *t.shape[3:])

    return from_residues(o), from_residues(m_t), from_residues(l_t)

def _dilated_attention_mixer(x, cos, sin, w_qkv, w_o):
    bsz, s, _ = x.shape
    qkv = (x @ w_qkv).reshape(bsz, s, ATT_N_GROUPS, 3, ATT_HEADS_PER_GROUP, ATT_HEAD_DIM)
    outs, maxes, dens = [], [], []
    for g, (window, dilation) in enumerate(ATT_PATTERNS):
        q = _apply_partial_rope(qkv[:, :, g, 0], cos, sin)
        k = _apply_partial_rope(qkv[:, :, g, 1], cos, sin)
        o, m, l = _dilated_window_attention(q, k, qkv[:, :, g, 2], window, dilation)
        outs.append(o)
        maxes.append(m)
        dens.append(l)
    o = jnp.stack(outs)
    m = jnp.stack(maxes)
    l = jnp.stack(dens)
    wgt = l * jnp.exp(m - jnp.max(m, 0, keepdims=True))
    merged = jnp.sum(wgt[..., None] * o, 0) / jnp.sum(wgt, 0)[..., None]
    return merged.reshape(bsz, s, ATT_OUT_DIM).astype(x.dtype) @ w_o

def _hierarchical_moe(x, w_rg, b_rg, w_re, b_re, w_gate, w_up, w_down):
    bsz, s, d = x.shape
    t = bsz * s
    xf = x.reshape(t, d)
    g_logits = (xf @ w_rg + b_rg).astype(jnp.float32)
    g_w, g_idx = lax.top_k(jax.nn.softmax(g_logits, axis=-1), 1)
    e_logits = (xf @ w_re + b_re).astype(jnp.float32).reshape(t, MOE_N_GROUPS, MOE_EXPERTS_PER_GROUP)
    e_logits = e_logits[jnp.arange(t), g_idx[:, 0]]
    e_w, e_idx = lax.top_k(jax.nn.softmax(e_logits, axis=-1), MOE_TOP_K)
    e_w = e_w / jnp.sum(e_w, -1, keepdims=True)
    gates = (g_w * e_w).reshape(-1)
    expert_id = (g_idx * MOE_EXPERTS_PER_GROUP + e_idx).reshape(-1).astype(jnp.int32)
    token_id = jnp.repeat(jnp.arange(t, dtype=jnp.int32), MOE_TOP_K)
    n_assign = t * MOE_TOP_K
    n_blocks = -(-n_assign // MOE_BLOCK) + MOE_N_EXPERTS
    n_rows = n_blocks * MOE_BLOCK
    order = jnp.argsort(expert_id)
    sorted_e = expert_id[order]
    counts = jnp.bincount(expert_id, length=MOE_N_EXPERTS)
    padded = (counts + MOE_BLOCK - 1) // MOE_BLOCK * MOE_BLOCK
    pad_end = jnp.cumsum(padded)
    pad_start = pad_end - padded
    cnt_start = jnp.cumsum(counts) - counts
    dest = pad_start[sorted_e] + jnp.arange(n_assign, dtype=jnp.int32) - cnt_start[sorted_e]
    row_tok = jnp.full((n_rows,), t, jnp.int32).at[dest].set(token_id[order])
    row_gate = jnp.zeros((n_rows,), x.dtype).at[dest].set(gates[order].astype(x.dtype))
    block_e = jnp.minimum(jnp.searchsorted(pad_end, jnp.arange(n_blocks) * MOE_BLOCK, side='right'),
                          MOE_N_EXPERTS - 1)
    x_rows = jnp.concatenate([xf, jnp.zeros((1, d), x.dtype)], 0)[row_tok]
    x_rows = x_rows.reshape(n_blocks, MOE_BLOCK, d)

    def expert_block(args):
        xb, e = args
        h = jax.nn.silu(xb @ w_gate[e]) * (xb @ w_up[e])
        return h @ w_down[e]

    y_rows = lax.map(expert_block, (x_rows, block_e)).reshape(n_rows, d)
    y = jax.ops.segment_sum(y_rows * row_gate[:, None], row_tok, num_segments=t + 1)[:t]
    return y.reshape(bsz, s, d)

def second_inputs(seed: int = 0) -> dict:
    key = jax.random.key(seed)
    ks = jax.random.split(key, 24)
    f32 = jnp.float32
    n_ssd = len(range(0, DEPTH, N_MIXERS_2))
    n_att = len(range(1, DEPTH, N_MIXERS_2))

    def nrm(k, shape, scale):
        return jax.random.normal(k, shape, f32) * scale

    x = jax.random.normal(ks[0], (BATCH, SEQ, D_MODEL), f32)
    positions = jnp.broadcast_to(jnp.arange(SEQ, dtype=jnp.int32), (BATCH, SEQ))
    dt0 = jnp.exp(jax.random.uniform(ks[4], (n_ssd, SSD_N_HEADS), f32) * (np.log(0.1) - np.log(0.001)) + np.log(0.001))
    return {
        'x': x,
        'positions': positions,
        'ssd_w_in': nrm(ks[1], (n_ssd, D_MODEL, SSD_D_IN_PROJ), D_MODEL ** -0.5),
        'ssd_conv_w': nrm(ks[2], (n_ssd, SSD_D_CONV, SSD_CONV_DIM), SSD_D_CONV ** -0.5),
        'ssd_conv_b': nrm(ks[3], (n_ssd, SSD_CONV_DIM), 0.02),
        'ssd_dt_bias': dt0 + jnp.log(-jnp.expm1(-dt0)),
        'ssd_a_log': jnp.log(jax.random.uniform(ks[5], (n_ssd, SSD_N_HEADS), f32, 1.0, 16.0)),
        'ssd_d': 1.0 + nrm(ks[6], (n_ssd, SSD_N_HEADS), 0.01),
        'ssd_norm_w': 1.0 + nrm(ks[7], (n_ssd, SSD_D_INNER), 0.02),
        'ssd_w_out': nrm(ks[8], (n_ssd, SSD_D_INNER, D_MODEL), SSD_D_INNER ** -0.5 * DEEPNORM_BETA_2),
        'attn_w_qkv': nrm(ks[9], (n_att, D_MODEL, ATT_QKV_DIM), D_MODEL ** -0.5),
        'attn_w_o': nrm(ks[10], (n_att, ATT_OUT_DIM, D_MODEL), ATT_OUT_DIM ** -0.5 * DEEPNORM_BETA_2),
        'ln_g': 1.0 + nrm(ks[11], (DEPTH, 2, D_MODEL), 0.02),
        'ln_b': nrm(ks[12], (DEPTH, 2, D_MODEL), 0.02),
        'moe_w_router_group': nrm(ks[13], (DEPTH, D_MODEL, MOE_N_GROUPS), D_MODEL ** -0.5),
        'moe_b_router_group': nrm(ks[14], (DEPTH, MOE_N_GROUPS), 0.01),
        'moe_w_router_expert': nrm(ks[15], (DEPTH, D_MODEL, MOE_N_EXPERTS), D_MODEL ** -0.5),
        'moe_b_router_expert': nrm(ks[16], (DEPTH, MOE_N_EXPERTS), 0.01),
        'moe_w_gate': nrm(ks[17], (DEPTH, MOE_N_EXPERTS, D_MODEL, MOE_HIDDEN), D_MODEL ** -0.5),
        'moe_w_up': nrm(ks[18], (DEPTH, MOE_N_EXPERTS, D_MODEL, MOE_HIDDEN), D_MODEL ** -0.5),
        'moe_w_down': nrm(ks[19], (DEPTH, MOE_N_EXPERTS, MOE_HIDDEN, D_MODEL), MOE_HIDDEN ** -0.5 * DEEPNORM_BETA_2),
    }

def second_block(x, positions, ssd_w_in, ssd_conv_w, ssd_conv_b, ssd_dt_bias, ssd_a_log, ssd_d,
              ssd_norm_w, ssd_w_out, attn_w_qkv, attn_w_o, ln_g, ln_b,
              moe_w_router_group, moe_b_router_group, moe_w_router_expert, moe_b_router_expert,
              moe_w_gate, moe_w_up, moe_w_down):
    cos, sin = _rope_tables(positions)
    for i in range(DEPTH):
        j = i // N_MIXERS_2
        if i % N_MIXERS_2 == 0:
            mix = _ssd_mixer(x, ssd_w_in[j], ssd_conv_w[j], ssd_conv_b[j], ssd_dt_bias[j],
                             ssd_a_log[j], ssd_d[j], ssd_norm_w[j], ssd_w_out[j])
        else:
            mix = _dilated_attention_mixer(x, cos, sin, attn_w_qkv[j], attn_w_o[j])
        x = _layer_norm_2(DEEPNORM_ALPHA_2 * x + mix, ln_g[i, 0], ln_b[i, 0])
        ffn = _hierarchical_moe(x, moe_w_router_group[i], moe_b_router_group[i],
                                moe_w_router_expert[i], moe_b_router_expert[i],
                                moe_w_gate[i], moe_w_up[i], moe_w_down[i])
        x = _layer_norm_2(DEEPNORM_ALPHA_2 * x + ffn, ln_g[i, 1], ln_b[i, 1])
    return x


def setup_inputs(seed=0):
    out = dict(first_inputs(seed))
    for name, value in second_inputs(seed + 1).items():
        if name != "x":
            out[name + "_2"] = value
    return out


def reference(
    x, c, ada_w, ada_b, ln_g, ln_b, ffn_w_in, ffn_w_out, rwkv_mu, rwkv_w_rkv, rwkv_w0, rwkv_w1,
    rwkv_w2, rwkv_a0, rwkv_a1, rwkv_a2, rwkv_g1, rwkv_g2, rwkv_k_k, rwkv_k_a, rwkv_r_k,
    rwkv_gn_g, rwkv_gn_b, rwkv_w_out, gdn_w_in, gdn_conv, gdn_a_log, gdn_dt_bias, gdn_norm_g,
    gdn_w_out, diff_w_in, diff_lambda, diff_subln_g, diff_w_out, swa_w_qkv, swa_b_qkv,
    swa_sinks, swa_w_out, swa_b_out, positions_2, ssd_w_in_2, ssd_conv_w_2, ssd_conv_b_2,
    ssd_dt_bias_2, ssd_a_log_2, ssd_d_2, ssd_norm_w_2, ssd_w_out_2, attn_w_qkv_2, attn_w_o_2,
    ln_g_2, ln_b_2, moe_w_router_group_2, moe_b_router_group_2, moe_w_router_expert_2,
    moe_b_router_expert_2, moe_w_gate_2, moe_w_up_2, moe_w_down_2,
):
    x = first_block(
        x, c, ada_w, ada_b, ln_g, ln_b, ffn_w_in, ffn_w_out, rwkv_mu, rwkv_w_rkv, rwkv_w0,
        rwkv_w1, rwkv_w2, rwkv_a0, rwkv_a1, rwkv_a2, rwkv_g1, rwkv_g2, rwkv_k_k, rwkv_k_a,
        rwkv_r_k, rwkv_gn_g, rwkv_gn_b, rwkv_w_out, gdn_w_in, gdn_conv, gdn_a_log, gdn_dt_bias,
        gdn_norm_g, gdn_w_out, diff_w_in, diff_lambda, diff_subln_g, diff_w_out, swa_w_qkv,
        swa_b_qkv, swa_sinks, swa_w_out, swa_b_out,
    )
    return second_block(
        x, positions_2, ssd_w_in_2, ssd_conv_w_2, ssd_conv_b_2, ssd_dt_bias_2, ssd_a_log_2,
        ssd_d_2, ssd_norm_w_2, ssd_w_out_2, attn_w_qkv_2, attn_w_o_2, ln_g_2, ln_b_2,
        moe_w_router_group_2, moe_b_router_group_2, moe_w_router_expert_2,
        moe_b_router_expert_2, moe_w_gate_2, moe_w_up_2, moe_w_down_2,
    )


_drawn_inputs = setup_inputs


def setup_inputs(seed=0):
    import zlib

    import numpy as np

    out = dict(_drawn_inputs(seed))
    spreads = {}
    factors = {'rwkv_w1': 5.496,
     'rwkv_w2': 5.271,
     'rwkv_a0': 3.896,
     'rwkv_gn_g': 6.497,
     'rwkv_gn_b': 7.539,
     'gdn_norm_g': 6.526,
     'ssd_conv_b_2': 3.652,
     'ssd_d_2': 8.0,
     'ssd_norm_w_2': 4.989,
     'moe_b_router_group_2': 8.0,
     'moe_b_router_expert_2': 8.0}
    for name, (base, spread) in spreads.items():
        noise = np.random.default_rng([zlib.crc32(name.encode()), seed]).standard_normal(out[name].shape)
        drawn = base * np.exp(spread * noise) if base else spread * noise
        out[name] = jnp.asarray(drawn.astype(out[name].dtype))
    for name, factor in factors.items():
        out[name] = (out[name] * factor).astype(out[name].dtype)
    return out
```

```python
import concourse.bass as bass
import numpy as np
from concourse import mybir
from concourse.alu_op_type import AluOpType as ALU
from contextlib import ExitStack

F32 = mybir.dt.float32
I32 = mybir.dt.int32
U32 = mybir.dt.uint32
ACT = mybir.ActivationFunctionType
AX = mybir.AxisListType

P = 128
T = 512
D = 1024
TT = T // P
DK = D // P
BANK = 512
LAYERS = 2
ALPHA = (2.0 * LAYERS) ** 0.25
LN_EPS = 1e-5
D_FF = ((8 * D + 3 * 256 - 1) // (3 * 256)) * 256
FK = D_FF // P
CH = 128
NC = T // CH

A_MU, A_W0, A_A0, A_KK, A_KA, A_RK, A_C = 0, 48, 56, 64, 72, 80, 88
A_ROWS = 96
GDN_HEADS = 8
CONV = 4
QKV_TILES = 3 * DK
SSD_TILES = 24


class Stage:

    def __init__(self, nc, name):
        self.nc, self.name, self.stack, self.sems = nc, name, ExitStack(), []

    def sb(self, name, shape, dt=F32):
        return self.stack.enter_context(self.nc.sbuf_tensor(f"{self.name}_{name}", shape, dt))

    def ps(self, name, shape, dt=F32):
        return self.stack.enter_context(self.nc.psum_tensor(f"{self.name}_{name}", shape, dt))

    def sem(self, name):
        s = self.stack.enter_context(self.nc.semaphore(f"{self.name}_{name}"))
        self.sems.append(s)
        return s

    def __enter__(self):
        return self

    def __exit__(self, kind, value, trace):
        if kind is None:
            ids = sorted(s.num for s in self.sems)
            at = 0
            while at < len(ids):
                to = at
                while to + 1 < len(ids) and ids[to + 1] == ids[to] + 1:
                    to += 1
                self.nc.gpsimd.sem_clear(range(ids[at], ids[to] + 1))
                at = to + 1
            self.nc.all_engine_barrier()
        self.stack.close()
        return False


class Chain:

    def __init__(self, eng, sem, start=0):
        self.eng, self.sem, self.n = eng, sem, start

    def __call__(self, ins):
        self.n = self.n + 1
        ins.then_inc(self.sem, 1)
        self.eng.wait_ge(self.sem, self.n)


def accumulate(nc, out, pairs):
    for i, (lhsT, rhs) in enumerate(pairs):
        last = nc.tensor.matmul(out, lhsT, rhs, start=(i == 0), stop=(i == len(pairs) - 1))
    return last


def row_broadcast(ap):
    return ap.rearrange("(a n) -> a n", a=1).to_broadcast([P, ap.shape[0]])


def constants_stage(nc, k, tables):
    with Stage(nc, "const") as st:
        rows = [st.sb(f"rows{i}", [P, P]) for i in range(3)]
        turned = st.ps("turned", [P, 3, BANK])
        loaded, ready, turned_done = st.sem("loaded"), st.sem("pool_step"), st.sem("turned_done")
        ones_done, copied = st.sem("ones_done"), st.sem("copied")
        with nc.Block() as block:
            @block.sync
            def _(sp):
                n = 0
                for i, parts in enumerate(tables):
                    at = 0
                    for part in parts:
                        sp.dma_start(rows[i][at:at + part.shape[0], :], part).then_inc(loaded, 16)
                        at += part.shape[0]
                        n += 1
                sp.wait_ge(loaded, 16 * n)

            @block.vector
            def _(dve):
                nc.vector.memset(k.ones[:, :], 1.0).then_inc(ones_done, 1)
                nc.vector.memset(k.ut[:, :, 0:1], 0.0).then_inc(ones_done, 1)
                for i, (dst, parts) in enumerate(zip((k.cola, k.colb, k.colc), tables)):
                    n = sum(p.shape[0] for p in parts)
                    dve.wait_ge(turned_done, i + 1)
                    nc.vector.tensor_copy(dst[:, 0:n], turned[:, i, 0:n]).then_inc(copied, 1)

            @block.gpsimd
            def _(pool):
                step = Chain(pool, ready)
                step(nc.gpsimd.memset(k.ident[:, :], 0.0))
                step(nc.gpsimd.affine_select(out=k.ident[:, :], in_=k.ident[:, :], compare_op=ALU.not_equal,
                                             fill=1.0, base=0, pattern=[[-1, P]], channel_multiplier=1))
                step(nc.gpsimd.memset(k.causal[:, :, :], 1.0))
                for i, base in enumerate((-1, 0)):
                    step(nc.gpsimd.affine_select(out=k.causal[:, i, :], in_=k.causal[:, i, :], compare_op=ALU.is_ge,
                                                 fill=0.0, base=base, pattern=[[1, P]], channel_multiplier=-1))
                step(nc.gpsimd.memset(k.per_head[:, :], 0.0))
                step(nc.gpsimd.memset(k.per_head[0:64, 0:64], 1.0))
                step(nc.gpsimd.memset(k.per_head[64:128, 64:128], 1.0))
                step(nc.gpsimd.memset(k.level[:, :, :], 1.0))
                for lv in range(7):
                    b = 1 << lv
                    g = P // (2 * b)
                    m = k.level[:, lv, :].rearrange("p (g r) -> p g r", g=g)
                    for base, pattern, cm in ((0, [[-2 * b, g], [0, 2 * b]], 1),
                                              (b - 1, [[2 * b, g], [0, 2 * b]], -1),
                                              (-b, [[0, g], [1, 2 * b]], 0)):
                        step(nc.gpsimd.affine_select(out=m, in_=m, compare_op=ALU.is_ge, fill=0.0, base=base,
                                                     pattern=pattern, channel_multiplier=cm))

            @block.tensor
            def _(pe):
                n = 0
                pe.wait_ge(ready, 2)
                for i, parts in enumerate(tables):
                    pe.wait_ge(loaded, 16 * sum(len(t) for t in tables))
                    n = sum(p.shape[0] for p in parts)
                    nc.tensor.transpose(turned[:, i, 0:n], rows[i][0:n, :], k.ident[0:n, 0:n]).then_inc(turned_done, 1)


def ada_stage(nc, k, ada_w, ada_b, ga_dram):
    CW = 512
    CHUNKS = 6 * D // CW
    RING = 3
    with Stage(nc, "ada") as st:
        ring = st.sb("ring", [P, RING, DK, CW])
        bias = st.sb("bias", [P, 6 * D])
        acc = st.sb("acc", [P, 2, CW])
        cond = st.sb("cond", [P, DK])
        sig = st.sb("sig", [P, DK])
        gate = st.sb("gate", [1, 2, CW])
        sums = st.ps("sums", [P, 2, BANK])
        loaded = [st.sem(f"loaded{i}") for i in range(RING)]
        bias_in, freed, cond_done, zeroed = st.sem("bias_in"), st.sem("freed"), st.sem("cond_done"), st.sem("zeroed")
        acc_done, summed, taken, stored, dstep = (st.sem("acc_done"), st.sem("summed"), st.sem("taken"),
                                                  st.sem("stored"), st.sem("dve_step"))
        bias_used = st.sem("bias_used")
        ROW = (4, 5, 10, 11)
        with nc.Block() as block:
            @block.sync
            def _(sp):
                sp.wait_ge(zeroed, 1)
                for l in range(LAYERS):
                    if l:
                        sp.wait_ge(bias_used, l)
                    sp.dma_start(bias[0:1, :], ada_b[l:l + 1, :]).then_inc(bias_in, 16)
                    w = ada_w[l].rearrange("(k p) n -> p k n", p=P)
                    for c in range(CHUNKS):
                        n = l * CHUNKS + c
                        if n >= RING:
                            sp.wait_ge(freed, n - RING + 1)
                        sp.dma_start(ring[:, n % RING, :, :], w[:, :, c * CW:(c + 1) * CW]).then_inc(loaded[n % RING], 16)

            @block.scalar
            def _(act):
                act.activation(sig[:, :], k.cola[:, A_C:A_C + DK], ACT.Sigmoid).then_inc(cond_done, 1)
                act.wait_ge(cond_done, 1)
                r = 0
                for l in range(LAYERS):
                    for c in range(CHUNKS):
                        n = l * CHUNKS + c
                        act.wait_ge(summed, n + 1)
                        if c in ROW:
                            if r:
                                act.wait_ge(stored, 16 * r)
                            act.activation(gate[0:1, r % 2, :], sums[0:1, n % 2, :], ACT.Copy, bias=1.0).then_inc(taken, 1)
                            act.wait_ge(taken, n + 1)
                            act.dma_start(ga_dram[l, c // 6, (c % 2) * CW:(c % 2 + 1) * CW].rearrange("(a n) -> a n", a=1),
                                          gate[0:1, r % 2, :]).then_inc(stored, 16)
                            r += 1
                        else:
                            part = (c // 6) * 2 + (c % 6) // 2
                            act.activation(k.modc[:, l, part, (c % 2) * 4:(c % 2) * 4 + 4], sums[:, n % 2, 0:4],
                                           ACT.Copy, bias=float(part % 2)).then_inc(taken, 1)
                act.wait_ge(stored, 16 * r)

            @block.vector
            def _(dve):
                nc.vector.memset(bias[:, :], 0.0).then_inc(zeroed, 1)
                step = Chain(dve, dstep)
                dve.wait_ge(cond_done, 1)
                step(nc.vector.tensor_tensor(cond[:, :], sig[:, :], k.cola[:, A_C:A_C + DK], ALU.mult))
                for l in range(LAYERS):
                    dve.wait_ge(bias_in, 16 * (l + 1))
                    for c in range(CHUNKS):
                        n = l * CHUNKS + c
                        a = acc[:, n % 2, :]
                        if n >= 2:
                            dve.wait_ge(summed, n - 1)
                        dve.wait_ge(loaded[n % RING], 16 * (n // RING + 1))
                        for kt in range(DK):
                            src = bias[:, c * CW:(c + 1) * CW] if kt == 0 else a
                            ins = nc.vector.scalar_tensor_tensor(a, ring[:, n % RING, kt, :], cond[:, kt:kt + 1], src,
                                                                 ALU.mult, ALU.add)
                            if kt < DK - 1:
                                step(ins)
                        ins.then_inc(acc_done, 1)
                        dve.wait_ge(acc_done, n + 1)
                        dve.sem_inc(freed, 1)
                    dve.sem_inc(bias_used, 1)

            @block.tensor
            def _(pe):
                for n in range(LAYERS * CHUNKS):
                    pe.wait_ge(acc_done, n + 1)
                    if n >= 2:
                        pe.wait_ge(taken, n - 1)
                    if n % CHUNKS in ROW:
                        last = nc.tensor.matmul(sums[0:1, n % 2, :], k.ones[:, 0:1], acc[:, n % 2, :], start=True, stop=True)
                    else:
                        for m in range(4):
                            last = nc.tensor.matmul(sums[:, n % 2, m:m + 1], acc[:, n % 2, m * P:(m + 1) * P],
                                                    k.ones[:, 0:1], start=True, stop=True)
                    last.then_inc(summed, 1)


def turn_stage(nc, k, name, scale=None, shift=None):
    with Stage(nc, name) as st:
        ps = st.ps("ps", [P, 4, BANK])
        turned, taken_a, taken_d = st.sem("turned"), st.sem("taken_by_act"), st.sem("taken_by_dve")
        with nc.Block() as block:
            @block.tensor
            def _(pe):
                for g in range(TT * 2):
                    tt, half = g // 2, g % 2
                    if g >= 4:
                        (pe.wait_ge(taken_a, (g - 4) // 2 + 1) if g % 2 == 0 else pe.wait_ge(taken_d, (g - 4) // 2 + 1))
                    for m in range(4):
                        d = half * 4 + m
                        last = nc.tensor.transpose(ps[:, g % 4, m * P:(m + 1) * P], k.x[:, tt, d * P:(d + 1) * P],
                                                   k.ident[:, :])
                    last.then_inc(turned, 1)

            def take(eng, half, taken):
                for g in range(half, TT * 2, 2):
                    tt = g // 2
                    eng.wait_ge(turned, g + 1)
                    if scale is None:
                        dst = k.ut[:, half * 4:half * 4 + 4, 1 + tt * P:1 + (tt + 1) * P]
                        src = ps[:, g % 4, :].rearrange("p (m t) -> p m t", m=4)
                        if half:
                            last = nc.vector.tensor_copy(dst, src)
                        else:
                            last = nc.scalar.activation(dst, src, ACT.Copy)
                    else:
                        for m in range(4):
                            d = half * 4 + m
                            dst, src = k.ut[:, d, 1 + tt * P:1 + (tt + 1) * P], ps[:, g % 4, m * P:(m + 1) * P]
                            if half:
                                last = nc.vector.tensor_scalar(dst, src, scale[:, d:d + 1], shift[:, d:d + 1], ALU.mult, ALU.add)
                            else:
                                last = nc.scalar.activation(dst, src, ACT.Identity, bias=shift[:, d:d + 1], scale=scale[:, d:d + 1])
                    last.then_inc(taken, 1)

            @block.scalar
            def _(act):
                take(act, 0, taken_a)

            @block.vector
            def _(dve):
                take(dve, 1, taken_d)


class Norm:

    def __init__(self, nc, k, st, ga, g, b):
        self.nc, self.k, self.ga, self.g, self.b = nc, k, ga, g, b
        self.tmp, self.stats, self.mv = st.sb("norm_tmp", [P, 2, BANK]), st.sb("norm_stats", [P, TT, 2, 6]), st.sb("norm_mv", [P, TT, 2])
        self.root, self.scaled = st.sb("norm_root", [P, TT]), st.sb("norm_scaled", [P, D])
        self.var_done, self.root_done = st.sem("var_done"), st.sem("root_done")

    def sums(self, step, tt, ys):
        nc, x = self.nc, self.k.x
        for h, y in enumerate(ys):
            s = slice(h * BANK, (h + 1) * BANK)
            if self.ga is not None:
                step(nc.vector.tensor_tensor(self.tmp[:, h, :], y, self.ga[:, s], ALU.mult))
                y = self.tmp[:, h, :]
            step(nc.vector.scalar_tensor_tensor(x[:, tt, s], x[:, tt, s], ALPHA, y, ALU.mult, ALU.add))
            step(nc.vector.bn_stats(self.stats[:, tt, h, :], x[:, tt, s]))
        step(nc.vector.bn_aggr(self.mv[:, tt, :], self.stats[:, tt, :, :]))

    def square_root(self, act):
        act.wait_ge(self.var_done, 1)
        act.activation(self.root[:, :], self.root[:, :], ACT.Sqrt).then_inc(self.root_done, 1)

    def finish(self, dve, step):
        nc, x = self.nc, self.k.x
        nc.vector.tensor_scalar(self.root[:, :], self.mv[:, :, 1], LN_EPS, None, ALU.add).then_inc(self.var_done, 1)
        dve.wait_ge(self.root_done, 1)
        step(nc.vector.reciprocal(self.root[:, :], self.root[:, :]))
        for tt in range(TT):
            step(nc.vector.tensor_scalar(self.scaled[:, :], x[:, tt, :], self.mv[:, tt, 0:1], self.root[:, tt:tt + 1],
                                         ALU.subtract, ALU.mult))
            step(nc.vector.tensor_tensor(self.scaled[:, :], self.scaled[:, :], self.g[:, :], ALU.mult))
            step(nc.vector.tensor_tensor(x[:, tt, :], self.scaled[:, :], self.b[:, :], ALU.add))


def project_norm_stage(nc, k, name, h, n_k, w, ga_row, ln_g, ln_b):
    RING, PER = 4, 2
    loads = n_k // PER
    with Stage(nc, name) as st:
        ring = st.sb("ring", [P, RING, PER, D])
        g, b = st.sb("g", [P, D]), st.sb("b", [P, D])
        ga = st.sb("ga", [P, D]) if ga_row is not None else None
        norm = Norm(nc, k, st, ga, g, b)
        y = st.ps("y", [P, TT, 2, BANK])
        loaded = [st.sem(f"loaded{i}") for i in range(RING)]
        rows_in, used, made, dstep = st.sem("rows_in"), st.sem("used"), st.sem("made"), st.sem("dve_step")
        wv = w.rearrange("(k p) n -> p k n", p=P)
        with nc.Block() as block:
            @block.sync
            def _(sp):
                for n in range(loads):
                    if n >= RING:
                        sp.wait_ge(used, n - RING + 1)
                    sp.dma_start(ring[:, n % RING, :, :], wv[:, n * PER:(n + 1) * PER, :]).then_inc(loaded[n % RING], 16)

            @block.scalar
            def _(act):
                act.dma_start(g[:, :], row_broadcast(ln_g)).then_inc(rows_in, 16)
                act.dma_start(b[:, :], row_broadcast(ln_b)).then_inc(rows_in, 16)
                if ga is not None:
                    act.dma_start(ga[:, :], row_broadcast(ga_row)).then_inc(rows_in, 16)
                act.wait_ge(rows_in, 48 if ga is not None else 32)
                norm.square_root(act)

            @block.tensor
            def _(pe):
                for n in range(loads):
                    pe.wait_ge(loaded[n % RING], 16 * (n // RING + 1))
                    for tt in range(TT):
                        for q in range(PER):
                            kk = n * PER + q
                            for half in range(2):
                                last = nc.tensor.matmul(y[:, tt, half, :], h[:, kk, tt * P:(tt + 1) * P],
                                                        ring[:, n % RING, q, half * BANK:(half + 1) * BANK],
                                                        start=(kk == 0), stop=(kk == n_k - 1))
                        if n == loads - 1:
                            last.then_inc(made, 1)
                    if n < loads - 1:
                        last.then_inc(used, 1)

            @block.vector
            def _(dve):
                step = Chain(dve, dstep)
                dve.wait_ge(rows_in, 48 if ga is not None else 32)
                for tt in range(TT):
                    dve.wait_ge(made, tt + 1)
                    norm.sums(step, tt, [y[:, tt, half, :] for half in range(2)])
                norm.finish(dve, step)


def ffn_stages(nc, k, l, w_in, w_out, ga_row, ln_g, ln_b):
    CW = 256
    CHUNKS = D_FF // CW
    with Stage(nc, f"ffn{l}") as outer:
        h = outer.sb("h", [P, FK, T])
        with Stage(nc, f"ffn_in{l}") as st:
            ring = st.sb("ring", [P, 2, 2, DK, CW])
            act_out = st.sb("act_out", [P, 2, T])
            ps = st.ps("ps", [P, 2, 2, BANK])
            loaded = [st.sem(f"loaded{i}") for i in range(2)]
            made, silu_done, h_done = st.sem("made"), st.sem("silu_done"), st.sem("h_done")
            wv = w_in.rearrange("(k p) (two n) -> p two k n", p=P, two=2)
            with nc.Block() as block:
                @block.sync
                def _(sp):
                    def load(c, slot):
                        for side in range(2):
                            sp.dma_start(ring[:, slot, side, :, :], wv[:, side, :, bass.ds(c * CW, CW)]).then_inc(loaded[slot], 16)

                    load(0, 0)
                    load(1, 1)
                    with sp.Fori(1, CHUNKS // 2) as i:
                        for slot in range(2):
                            sp.wait_ge(made, 4 * i + 2 * slot - 2)
                            load(2 * i + slot, slot)
                    sp.wait_ge(made, 2 * (CHUNKS - 2))
                    load(CHUNKS - 1, 0)

                @block.tensor
                def _(pe):
                    def tile(f, slot, m, first=False):
                        if not first:
                            pe.wait_ge(h_done, f - 1)
                        for side in range(2):
                            last = accumulate(nc, ps[:, m, side, :],
                                              [(ring[:, slot, side, kk, m * P:(m + 1) * P], k.ut[:, kk, 1:T + 1]) for kk in range(DK)])
                        last.then_inc(made, 1)

                    def chunk(c, slot, first=False):
                        for m in range(2):
                            tile(2 * c + m, slot, m, first)

                    pe.wait_ge(loaded[0], 32)
                    chunk(0, 0, True)
                    pe.wait_ge(loaded[1], 32)
                    chunk(1, 1)
                    with pe.Fori(1, CHUNKS // 2) as i:
                        for slot in range(2):
                            pe.wait_ge(loaded[slot], 32 * i + 32)
                            chunk(2 * i + slot, slot)
                    pe.wait_ge(loaded[0], 32 * (CHUNKS // 2 + 1))
                    chunk(CHUNKS - 1, 0)

                @block.scalar
                def _(act):
                    def tile(f, m, first=False):
                        if not first:
                            act.wait_ge(h_done, f - 1)
                        act.wait_ge(made, f + 1)
                        act.activation(act_out[:, m, :], ps[:, m, 0, :], ACT.Silu).then_inc(silu_done, 1)

                    tile(0, 0, True)
                    tile(1, 1, True)
                    with act.Fori(1, FK // 2) as i:
                        for m in range(2):
                            tile(2 * i + m, m)

                @block.vector
                def _(dve):
                    with dve.Fori(0, FK // 2) as i:
                        for m in range(2):
                            f = 2 * i + m
                            dve.wait_ge(silu_done, f + 1)
                            nc.vector.tensor_tensor(h[:, bass.ds(f, 1), :], act_out[:, m:m + 1, :], ps[:, m, 1:2, :],
                                                    ALU.mult).then_inc(h_done, 1)
        project_norm_stage(nc, k, f"ffn_out{l}", h, FK, w_out, ga_row, ln_g, ln_b)


RWKV_HEADS, HD = 16, 64
RWKV_GN_EPS = 64e-5
RWKV_DECAY = -float(np.exp(-0.5))


def inverse_stage(nc, k, name, lt, n_items):
    LEVELS = 7
    W = 4 * P
    with Stage(nc, name) as st:
        ltm = st.sb("ltm", [P, 2, 2, W])
        src = st.sb("src", [P, 2, W])
        lx = st.sb("lx", [P, 2, W])
        t = st.sb("t", [P, 2, W])
        tt_ = st.sb("tt", [P, 2, W])
        px, pz, pzt = st.ps("px", [P, 2, BANK]), st.ps("pz", [P, 2, BANK]), st.ps("pzt", [P, 2, BANK])
        src_in, masked, x_made, x_taken = st.sem("src_in"), st.sem("masked"), st.sem("x_made"), st.sem("x_taken")
        z_made, joined, zt_made, dstep, written = (st.sem("z_made"), st.sem("joined"), st.sem("zt_made"),
                                                   st.sem("dve_step"), st.sem("written"))
        N = n_items // 2
        q4 = lambda ap: ap.rearrange("p (h t) -> p h t", h=4)
        with nc.Block() as block:
            @block.gpsimd
            def _(pool):
                with pool.Fori(0, N) as i:
                    for lv in range(LEVELS):
                        for s in range(2):
                            n = i * (2 * LEVELS) + (2 * lv + s)
                            if lv == 0:
                                pool.wait_ge(src_in, 2 * i + s + 1)
                            if lv >= 2:
                                pool.wait_ge(x_made, n - 3)
                            m = k.level[:, lv:lv + 1, :].to_broadcast([P, 4, P])
                            nc.gpsimd.tensor_tensor(q4(ltm[:, s, lv % 2, :]), q4(src[:, s, :]), m, ALU.mult).then_inc(masked, 1)

            @block.tensor
            def _(pe):
                with pe.Fori(0, N) as i:
                    for lv in range(LEVELS):
                        for s in range(2):
                            n = i * (2 * LEVELS) + (2 * lv + s)
                            pe.wait_ge(masked, n + 1)
                            pe.wait_ge(joined, i * (2 * LEVELS + 2) + (2 * lv + s + 1))
                            for h in range(4):
                                last = nc.tensor.matmul(px[:, s, h * P:(h + 1) * P], ltm[:, s, lv % 2, h * P:(h + 1) * P],
                                                        t[:, s, h * P:(h + 1) * P], start=True, stop=True)
                            last.then_inc(x_made, 1)
                        for s in range(2):
                            n = i * (2 * LEVELS) + (2 * lv + s)
                            pe.wait_ge(x_taken, n + 1)
                            if lv < LEVELS - 1:
                                for h in range(4):
                                    last = nc.tensor.matmul(pz[:, s, h * P:(h + 1) * P], tt_[:, s, h * P:(h + 1) * P],
                                                            lx[:, s, h * P:(h + 1) * P], start=True, stop=True)
                                last.then_inc(z_made, 1)
                            for h in range(4):
                                last = nc.tensor.matmul(pzt[:, s, h * P:(h + 1) * P], lx[:, s, h * P:(h + 1) * P],
                                                        tt_[:, s, h * P:(h + 1) * P], start=True, stop=True)
                            last.then_inc(zt_made, 1)

            @block.scalar
            def _(act):
                with act.Fori(0, N) as i:
                    for s in range(2):
                        act.wait_ge(joined, i * (2 * LEVELS + 2) + s + 1)
                        act.activation(src[:, s:s + 1, :], lt[:, bass.ds(2 * i + s, 1), :], ACT.Copy).then_inc(src_in, 1)
                    for lv in range(LEVELS):
                        for s in range(2):
                            n = i * (2 * LEVELS) + (2 * lv + s)
                            act.wait_ge(x_made, n + 1)
                            act.activation(lx[:, s, :], px[:, s, :], ACT.Copy).then_inc(x_taken, 1)

            @block.vector
            def _(dve):
                identity = k.ident[:, :].rearrange("p (a t) -> p a t", a=1).to_broadcast([P, 4, P])
                with dve.Fori(0, N) as i:
                    for s in range(2):
                        nc.vector.tensor_copy(q4(t[:, s, :]), identity).then_inc(dstep, 1)
                        nc.vector.tensor_copy(q4(tt_[:, s, :]), identity).then_inc(joined, 1)
                    for lv in range(LEVELS - 1):
                        for s in range(2):
                            n = i * (2 * LEVELS) + (2 * lv + s)
                            dve.wait_ge(z_made, i * (2 * LEVELS - 2) + (2 * lv + s + 1))
                            dve.wait_ge(zt_made, n + 1)
                            nc.vector.tensor_tensor(t[:, s, :], t[:, s, :], pz[:, s, :], ALU.add).then_inc(dstep, 1)
                            nc.vector.tensor_tensor(tt_[:, s, :], tt_[:, s, :], pzt[:, s, :], ALU.add).then_inc(joined, 1)
                    for s in range(2):
                        n = i * (2 * LEVELS) + (2 * (LEVELS - 1) + s)
                        dve.wait_ge(zt_made, n + 1)
                        nc.vector.tensor_tensor(lt[:, bass.ds(2 * i + s, 1), :], tt_[:, s:s + 1, :], pzt[:, s:s + 1, :],
                                                ALU.add).then_inc(joined, 1)
                    dve.wait_ge(joined, (2 * LEVELS + 2) * i + (2 * LEVELS + 2))


def rwkv_stages(nc, k, p, ga_row, ln_g, ln_b, gn_g_row, gn_b_row):
    with Stage(nc, "rwkv") as outer:
        ar = outer.sb("ar", [P, DK, 2, T])
        bh = outer.sb("bh", [P, DK, T])
        kh = outer.sb("kh", [P, DK, T])
        v = outer.sb("v", [P, TT, D])
        carry = outer.sb("carry", [P, DK, NC])
        bonus = outer.sb("bonus", [P, TT, RWKV_HEADS])
        with Stage(nc, "rwkv_proj") as st:
            CW, RING = 256, 2
            ring = st.sb("ring", [P, RING, DK, CW])
            mix = st.sb("mix", [P, 2, DK, T])
            diff = st.sb("diff", [P, 2, T])
            w1, a1 = st.sb("w1", [P, DK, HD]), st.sb("a1", [P, DK, HD])
            w2, a2 = st.sb("w2", [HD, D]), st.sb("a2", [HD, D])
            low = st.sb("low", [HD, 2, T])
            ps = st.ps("ps", [P, 8, BANK])
            loaded = [st.sem(f"loaded{i}") for i in range(RING)]
            lora_in, mixed, made, taken, dstep = (st.sem("lora_in"), st.sem("mixed"), st.sem("made"), st.sem("taken"),
                                                  st.sem("dve_step"))
            with nc.Block() as block:
                @block.sync
                def _(sp):
                    n = 0
                    for i in range(3):
                        wv = p["w_rkv"][i].rearrange("(k p) n -> p k n", p=P)
                        for c in range(D // CW):
                            if n >= RING:
                                sp.wait_ge(made, 2 * (n - RING + 1))
                            sp.dma_start(ring[:, n % RING, :, :], wv[:, :, c * CW:(c + 1) * CW]).then_inc(loaded[n % RING], 16)
                            n += 1

                @block.scalar
                def _(act):
                    act.dma_start(w1[:, :, :], p["w1"].rearrange("(k p) n -> p k n", p=P)).then_inc(lora_in, 16)
                    act.dma_start(a1[:, :, :], p["a1"].rearrange("(k p) n -> p k n", p=P)).then_inc(lora_in, 16)
                    act.dma_start(w2[:, :], p["w2"]).then_inc(lora_in, 16)
                    act.dma_start(a2[:, :], p["a2"]).then_inc(lora_in, 16)
                    for g in range(42):
                        act.wait_ge(made, g + 1)
                        src = ps[:, g % 8, :]
                        if g < 8:
                            ins = act.activation(ar[:, g, 1, :], src, ACT.Copy)
                        elif g < 16:
                            ins = act.activation(kh[:, g - 8, :], src, ACT.Copy)
                        elif g < 24:
                            c, q = (g - 16) // 2, g % 2
                            ins = act.activation(v[:, 2 * q:2 * q + 2, c * CW:(c + 1) * CW],
                                                 src.rearrange("p (a n) -> p a n", a=2), ACT.Copy)
                        elif g < 26:
                            ins = act.activation(low[:, g - 24, :], ps[0:HD, g % 8, :], (ACT.Tanh, ACT.Copy)[g - 24])
                        elif g < 34:
                            ins = act.activation(ar[:, g - 26, 0, :], src, ACT.Sigmoid, bias=k.cola[:, A_W0 + g - 26:A_W0 + g - 25])
                        else:
                            ins = act.activation(bh[:, g - 34, :], src, ACT.Sigmoid, bias=k.cola[:, A_A0 + g - 34:A_A0 + g - 33])
                        ins.then_inc(taken, 1)

                @block.vector
                def _(dve):
                    n = 0
                    for i in range(5):
                        if i >= 2:
                            dve.wait_ge(made, (8, 16, 24)[i - 2])
                        for j in range(DK):
                            nc.vector.tensor_tensor(diff[:, n % 2, :], k.ut[:, j, 0:T], k.ut[:, j, 1:T + 1], ALU.subtract).then_inc(dstep, 1)
                            n += 1
                            dve.wait_ge(dstep, n)
                            nc.vector.scalar_tensor_tensor(mix[:, i % 2, j, :], diff[:, (n - 1) % 2, :],
                                                           k.cola[:, A_MU + i * DK + j:A_MU + i * DK + j + 1],
                                                           k.ut[:, j, 1:T + 1], ALU.mult, ALU.add).then_inc(mixed, 1)

                @block.tensor
                def _(pe):
                    for g in range(42):
                        if g >= 8:
                            pe.wait_ge(taken, g - 7)
                        dst = ps[:, g % 8, :]
                        if g < 24:
                            c = g // 2
                            if g % 2 == 0:
                                pe.wait_ge(loaded[c % RING], 16 * (c // RING + 1))
                        if g in (0, 8, 16, 24, 25):
                            pe.wait_ge(mixed, DK * {0: 1, 8: 2, 16: 3, 24: 4, 25: 5}[g])
                        if g < 16:
                            last = accumulate(nc, dst, [(ring[:, c % RING, kk, (g % 2) * P:(g % 2 + 1) * P], mix[:, g // 8, kk, :])
                                                        for kk in range(DK)])
                        elif g < 24:
                            for q in range(2):
                                tt = (g % 2) * 2 + q
                                last = accumulate(nc, ps[:, g % 8, q * CW:(q + 1) * CW],
                                                  [(mix[:, 0, kk, tt * P:(tt + 1) * P], ring[:, c % RING, kk, :]) for kk in range(DK)])
                        elif g < 26:
                            if g == 24:
                                pe.wait_ge(lora_in, 64)
                            w = (w1, a1)[g - 24]
                            last = accumulate(nc, ps[0:HD, g % 8, :], [(w[:, kk, :], mix[:, (g - 24 + 3) % 2, kk, :]) for kk in range(DK)])
                        else:
                            if g == 26:
                                pe.wait_ge(taken, 26)
                            w, m = ((w2, g - 26) if g < 34 else (a2, g - 34))
                            last = nc.tensor.matmul(dst, w[:, m * P:(m + 1) * P], low[:, (0 if g < 34 else 1), :], start=True, stop=True)
                        last.then_inc(made, 1)

        with Stage(nc, "rwkv_hat") as st:
            names = ("kk", "sq", "lw", "cum", "e_r", "e_k", "e_a", "prod")
            buf = {n: st.sb(n, [P, 2, T]) for n in names}
            inv_ka = st.sb("inv_ka", [P, DK])
            ends = st.sb("ends", [P, NC + 1])
            heads = st.sb("heads", [P, 2])
            inv_norm = st.sb("inv_norm", [P, DK, T])
            norm, bon = st.ps("norm", [P, 2, BANK]), st.ps("bon", [P, TT, RWKV_HEADS])
            norm_in, root_done = st.sem("norm_in"), st.sem("root_done")
            dstep, sq_done, norm_done, cum_done, exp_done, prod_done, bonus_done = (
                st.sem("dve_step"), st.sem("sq_done"), st.sem("norm_done"), st.sem("cum_done"), st.sem("exp_done"),
                st.sem("prod_done"), st.sem("bonus_done"))
            b4 = lambda ap: ap.rearrange("p (c t) -> p c t", c=NC)
            with nc.Block() as block:
                @block.vector
                def _(dve):
                    step = Chain(dve, dstep)
                    step(nc.vector.tensor_copy(heads[:, 0:1], k.per_head[:, 0:1]))
                    step(nc.vector.tensor_copy(heads[:, 1:2], k.per_head[:, 64:65]))
                    step(nc.vector.tensor_scalar(inv_ka[:, :], k.cola[:, A_KA:A_KA + DK], -1.0, 1.0, ALU.mult, ALU.add))
                    for j in range(DK + 1):
                        if j < DK:
                            kk, sq = buf["kk"][:, j % 2, :], buf["sq"][:, j % 2, :]
                            step(nc.vector.tensor_scalar(kk, kh[:, j, :], k.cola[:, A_KK + j:A_KK + j + 1], None, ALU.mult))
                            nc.vector.tensor_tensor(sq, kk, kk, ALU.mult).then_inc(sq_done, 1)
                        if j:
                            dve.wait_ge(norm_done, j)
                            nc.vector.tensor_scalar(inv_norm[:, j - 1, :], norm[:, (j - 1) % 2, :], 1e-6, None, ALU.add).then_inc(norm_in, 1)
                    dve.wait_ge(root_done, 1)
                    step(nc.vector.reciprocal(inv_norm[:, :, :], inv_norm[:, :, :]))
                    for j in range(DK):
                        kk, sq, lw, cum, er, ek, ea, prod = (buf[n][:, j % 2, :] for n in names)
                        col = lambda a: k.cola[:, a + j:a + j + 1]
                        if j >= 2:
                            dve.wait_ge(bonus_done, j - 1)
                        step(nc.vector.scalar_tensor_tensor(kk, kh[:, j, :], col(A_KK), inv_norm[:, j, :], ALU.mult, ALU.mult))
                        step(nc.vector.tensor_scalar(lw, ar[:, j, 0, :], RWKV_DECAY, None, ALU.mult))
                        for c in range(NC):
                            s = slice(c * CH, (c + 1) * CH)
                            step(nc.vector.tensor_tensor_scan(cum[:, s], k.ones[:, :], lw[:, s], 0.0, ALU.mult, ALU.add))
                        step(nc.vector.tensor_copy(ends[:, 0:NC], b4(cum)[:, :, CH // 2 - 1]))
                        step(nc.vector.tensor_tensor(b4(cum), b4(cum), ends[:, 0:NC].unsqueeze(2).to_broadcast([P, NC, CH]), ALU.subtract))
                        step(nc.vector.tensor_tensor(carry[:, j, 0:NC - 1], b4(cum)[:, 0:NC - 1, CH - 1], ends[:, 1:NC], ALU.add))
                        nc.vector.tensor_tensor(lw, cum, lw, ALU.subtract).then_inc(cum_done, 1)
                        step(nc.vector.tensor_scalar(prod, bh[:, j, :], col(A_KA), inv_ka[:, j:j + 1], ALU.mult, ALU.add))
                        step(nc.vector.tensor_tensor(kh[:, j, :], kh[:, j, :], prod, ALU.mult))
                        nc.vector.scalar_tensor_tensor(prod, ar[:, j, 1, :], col(A_RK), kh[:, j, :], ALU.mult, ALU.mult).then_inc(prod_done, 1)
                        step(nc.vector.tensor_tensor(bh[:, j, :], bh[:, j, :], kk, ALU.mult))
                        dve.wait_ge(exp_done, j + 1)
                        step(nc.vector.tensor_tensor(bh[:, j, :], bh[:, j, :], ek, ALU.mult))
                        step(nc.vector.tensor_tensor(kh[:, j, :], kh[:, j, :], ek, ALU.mult))
                        step(nc.vector.tensor_tensor(ar[:, j, 1, :], ar[:, j, 1, :], er, ALU.mult))
                        step(nc.vector.scalar_tensor_tensor(ar[:, j, 0, :], kk, -1.0, ea, ALU.mult, ALU.mult))
                    dve.wait_ge(bonus_done, DK)
                    step(nc.vector.tensor_copy(bonus[:, :, :], bon[:, :, :]))

                @block.scalar
                def _(act):
                    act.wait_ge(norm_in, DK)
                    act.activation(inv_norm[:, :, :], inv_norm[:, :, :], ACT.Sqrt).then_inc(root_done, 1)
                    for j in range(DK):
                        kk, sq, lw, cum, er, ek, ea, prod = (buf[n][:, j % 2, :] for n in names)
                        act.wait_ge(cum_done, j + 1)
                        act.activation(er, cum, ACT.Exp)
                        act.activation(ek, cum, ACT.Exp, scale=-1.0)
                        act.activation(carry[:, j, 0:NC - 1], carry[:, j, 0:NC - 1], ACT.Exp)
                        act.activation(ea, lw, ACT.Exp).then_inc(exp_done, 1)

                @block.tensor
                def _(pe):
                    for j in range(DK):
                        pe.wait_ge(sq_done, j + 1)
                        if j >= 2:
                            pe.wait_ge(norm_in, j - 1)
                        nc.tensor.matmul(norm[:, j % 2, :], k.per_head[:, :], buf["sq"][:, j % 2, :], start=True, stop=True).then_inc(norm_done, 1)
                    for j in range(DK):
                        prod = buf["prod"][:, j % 2, :]
                        pe.wait_ge(prod_done, j + 1)
                        for tt in range(TT):
                            last = nc.tensor.matmul(bon[:, tt, 2 * j:2 * j + 2], prod[:, tt * P:(tt + 1) * P], heads[:, :],
                                                    start=True, stop=True)
                        last.then_inc(bonus_done, 1)

        with Stage(nc, "rwkv_rec") as rec:
            ITEMS, GR = NC * 4, 4
            lt = rec.sb("lt", [P, ITEMS, 4 * P])
            y = rec.sb("y", [P, TT, D])
            mask = k.causal[:, :, :].bitcast(I32)
            chunk = lambda c: slice(c * CH, (c + 1) * CH)
            with Stage(nc, "rwkv_low") as st:
                ps = st.ps("ps", [P, 2, 2, BANK])
                zeroed, made, taken = st.sem("zeroed"), st.sem("made"), st.sem("taken")
                with nc.Block() as block:
                    @block.gpsimd
                    def _(pool):
                        nc.gpsimd.memset(lt[:, :, :], 0.0).then_inc(zeroed, 1)

                    @block.tensor
                    def _(pe):
                        for n in range(ITEMS):
                            c, g = n // GR, n % GR
                            if n >= 2:
                                pe.wait_ge(taken, n - 1)
                            for pair in range(2):
                                for side in range(2):
                                    j, hb = 2 * g + pair, 64 * side
                                    last = nc.tensor.matmul(ps[:, n % 2, side, pair * P:(pair + 1) * P], bh[hb:hb + 64, j, chunk(c)],
                                                            ar[hb:hb + 64, j, 0, chunk(c)], start=True, stop=True)
                            last.then_inc(made, 1)

                    @block.vector
                    def _(dve):
                        dve.wait_ge(zeroed, 1)
                        for n in range(ITEMS):
                            dve.wait_ge(made, n + 1)
                            for side in range(2):
                                last = nc.vector.copy_predicated(lt[:, n, side * 2 * P:(side + 1) * 2 * P].rearrange("p (h t) -> p h t", h=2),
                                                                 mask[:, 0:1, :].to_broadcast([P, 2, P]),
                                                                 ps[:, n % 2, side, 0:2 * P].rearrange("p (h t) -> p h t", h=2))
                            last.then_inc(taken, 1)
            inverse_stage(nc, k, "rwkv_inv", lt, ITEMS)

            with Stage(nc, "rwkv_scan") as st:
                state = st.sb("state", [P, DK, HD])
                rb = st.sb("rb", [P, 2, 4 * P])
                ka = st.sb("ka", [P, 2, 2, 2, 2, P])
                tok = st.sb("tok", [P, 2, 4, P])
                rhs, u = st.sb("rhs", [P, 2, 4, HD]), st.sb("u", [P, 2, 4, HD])
                ps = st.ps("ps", [P, 8, BANK])
                names = ("zeroed", "ka_made", "ka_taken", "rb_made", "rb_taken", "tok_made", "tok_taken", "rhs_made", "rhs_taken",
                         "u_made", "u_taken", "y_made", "y_taken", "s_made", "s_taken", "dve_step")
                s = {n: st.sem(n) for n in names}
                p2 = lambda ap: ap.rearrange("p (h n) -> p h n", h=2)
                with nc.Block() as block:
                    @block.gpsimd
                    def _(pool):
                        nc.gpsimd.memset(rb[:, :, :], 0.0).then_inc(s["zeroed"], 1)
                        nc.gpsimd.memset(ka[:, :, :, :, :, :], 0.0).then_inc(s["zeroed"], 1)
                        nc.gpsimd.memset(state[:, :, :], 0.0).then_inc(s["zeroed"], 1)

                    @block.tensor
                    def _(pe):
                        pe.wait_ge(s["zeroed"], 3)
                        for n in range(ITEMS):
                            c, g, b = n // GR, n % GR, n % 2
                            hs = [(side, pair, 2 * g + pair, slice(64 * side, 64 * side + 64)) for pair in range(2) for side in range(2)]
                            if n >= 1:
                                pe.wait_ge(s["ka_taken"], n)
                            for side, pair, j, f in hs:
                                last = nc.tensor.matmul(ps[:, side, pair * 2 * P:(pair + 1) * 2 * P], kh[f, j, chunk(c)],
                                                        ar[f, j, :, chunk(c)], start=True, stop=True)
                            last.then_inc(s["ka_made"], 1)
                            if n >= 1:
                                pe.wait_ge(s["rhs_taken"], n)
                            for side, pair, j, f in hs:
                                last = nc.tensor.matmul(ps[:, 2 + side, pair * P:(pair + 1) * P], bh[f, j, chunk(c)],
                                                        ar[f, j, 1, chunk(c)], start=True, stop=True)
                            last.then_inc(s["rb_made"], 1)
                            if n >= 1:
                                pe.wait_ge(s["tok_taken"], n)
                            for pair in range(2):
                                for w, src in enumerate((bh, kh)):
                                    last = nc.tensor.transpose(ps[:, 7, (2 * w + pair) * P:(2 * w + pair + 1) * P],
                                                               src[:, 2 * g + pair, chunk(c)], k.ident[:, :])
                            last.then_inc(s["tok_made"], 1)
                            pe.wait_ge(s["ka_taken"], n + 1)
                            pe.wait_ge(s["rb_taken"], n + 1)
                            if n >= GR:
                                pe.wait_ge(s["s_taken"], n - GR + 1)
                            for side, pair, j, f in hs:
                                h = 2 * j + side
                                out = ps[:, 2 + side, 256 + pair * HD:256 + (pair + 1) * HD]
                                nc.tensor.matmul(out, ka[:, b, side, pair, 0, :], v[:, c, h * HD:(h + 1) * HD], start=True, stop=False)
                                last = nc.tensor.matmul(out, ar[f, j, 0, chunk(c)], state[f, j, :], start=False, stop=True)
                            last.then_inc(s["rhs_made"], 1)
                            pe.wait_ge(s["rhs_taken"], n + 1)
                            if n >= 1:
                                pe.wait_ge(s["s_taken"], n)
                            for side, pair, j, f in hs:
                                q = side * 2 + pair
                                last = nc.tensor.matmul(ps[:, 6, q * HD:(q + 1) * HD], lt[:, n, q * P:(q + 1) * P], rhs[:, b, q, :],
                                                        start=True, stop=True)
                            last.then_inc(s["u_made"], 1)
                            if n >= 1:
                                pe.wait_ge(s["y_taken"], n)
                            pe.wait_ge(s["u_taken"], n + 1)
                            for side, pair, j, f in hs:
                                h, q = 2 * j + side, side * 2 + pair
                                out = ps[:, 4 + side, pair * HD:(pair + 1) * HD]
                                nc.tensor.matmul(out, ka[:, b, side, pair, 1, :], v[:, c, h * HD:(h + 1) * HD], start=True, stop=False)
                                nc.tensor.matmul(out, rb[:, b, q * P:(q + 1) * P], u[:, b, q, :], start=False, stop=False)
                                last = nc.tensor.matmul(out, ar[f, j, 1, chunk(c)], state[f, j, :], start=False, stop=True)
                            last.then_inc(s["y_made"], 1)
                            pe.wait_ge(s["tok_taken"], n + 1)
                            for side, pair, j, f in hs:
                                h, q = 2 * j + side, side * 2 + pair
                                out = ps[f, 6, 256 + pair * HD:256 + (pair + 1) * HD]
                                nc.tensor.matmul(out, tok[:, b, pair, f], u[:, b, q, :], start=True, stop=False)
                                last = nc.tensor.matmul(out, tok[:, b, 2 + pair, f], v[:, c, h * HD:(h + 1) * HD], start=False, stop=True)
                            last.then_inc(s["s_made"], 1)

                    @block.scalar
                    def _(act):
                        for n in range(ITEMS):
                            c, g, b = n // GR, n % GR, n % 2
                            act.wait_ge(s["tok_made"], n + 1)
                            act.activation(tok[:, b, :, :], ps[:, 7, :].rearrange("p (a t) -> p a t", a=4), ACT.Copy).then_inc(s["tok_taken"], 1)
                            act.wait_ge(s["u_made"], n + 1)
                            act.activation(u[:, b, :, :], ps[:, 6, 0:256].rearrange("p (a t) -> p a t", a=4), ACT.Copy).then_inc(s["u_taken"], 1)
                            act.wait_ge(s["y_made"], n + 1)
                            for side in range(2):
                                dst = y[:, c, g * 256:(g + 1) * 256].rearrange("p (a s n) -> p s a n", a=2, s=2)[:, side, :, :]
                                last = act.activation(dst, p2(ps[:, 4 + side, 0:2 * HD]), ACT.Copy)
                            last.then_inc(s["y_taken"], 1)

                    @block.vector
                    def _(dve):
                        step = Chain(dve, s["dve_step"])
                        dve.wait_ge(s["zeroed"], 3)
                        for n in range(ITEMS):
                            c, g, b = n // GR, n % GR, n % 2
                            dve.wait_ge(s["ka_made"], n + 1)
                            for side in range(2):
                                for pair in range(2):
                                    last = nc.vector.copy_predicated(ka[:, b, side, pair, :, :], mask,
                                                                     p2(ps[:, side, pair * 2 * P:(pair + 1) * 2 * P]))
                            last.then_inc(s["ka_taken"], 1)
                            dve.wait_ge(s["rb_made"], n + 1)
                            for side in range(2):
                                last = nc.vector.copy_predicated(p2(rb[:, b, side * 2 * P:(side + 1) * 2 * P]),
                                                                 mask[:, 1:2, :].to_broadcast([P, 2, P]), p2(ps[:, 2 + side, 0:2 * P]))
                            last.then_inc(s["rb_taken"], 1)
                            dve.wait_ge(s["rhs_made"], n + 1)
                            for side in range(2):
                                last = nc.vector.tensor_copy(rhs[:, b, side * 2:side * 2 + 2, :], p2(ps[:, 2 + side, 256:256 + 2 * HD]))
                            last.then_inc(s["rhs_taken"], 1)
                            dve.wait_ge(s["s_made"], n + 1)
                            sl = state[:, 2 * g:2 * g + 2, :]
                            step(nc.vector.tensor_tensor(sl, sl, p2(ps[:, 6, 256:256 + 2 * HD]), ALU.add))
                            scale = carry[:, 2 * g:2 * g + 2, c:c + 1].to_broadcast([P, 2, HD]) if c < NC - 1 else None
                            if scale is not None:
                                nc.vector.tensor_tensor(sl, sl, scale, ALU.mult).then_inc(s["s_taken"], 1)
                            else:
                                nc.vector.tensor_copy(sl, sl).then_inc(s["s_taken"], 1)

            with Stage(nc, "rwkv_out") as st:
                CWG = 2
                g1, g2 = st.sb("g1", [P, DK, P]), st.sb("g2", [P, D])
                diff, mix = st.sb("diff", [P, 2, T]), ar[:, :, 0, :]
                sg = st.sb("sg", [P, T])
                gng, gnb = st.sb("gng", [P, D]), st.sb("gnb", [P, D])
                mean, var = (st.sb(n, [P, TT * RWKV_HEADS]) for n in ("mean", "var"))
                tmp = kh[:, :, :].rearrange("p k t -> p (k t)")
                low = st.ps("low", [P, BANK])
                gate = st.ps("gate", [P, 2, BANK])
                turned = st.ps("turned", [P, 2, BANK])
                names = ("loaded", "mixed", "low_made", "sg_done", "gate_made", "gate_taken", "y_done", "turn_made", "turn_taken",
                         "dve_step", "diff_done", "var_done", "root_done")
                s = {n: st.sem(n) for n in names}
                GH = TT * RWKV_HEADS
                hv = lambda ap: ap.rearrange("p (h n) -> p h n", h=GH)
                bc = lambda ap: ap.unsqueeze(2).to_broadcast([P, GH, HD])
                with nc.Block() as block:
                    @block.sync
                    def _(sp):
                        sp.dma_start(g1[:, :, :], p["g1"].rearrange("(k p) n -> p k n", p=P)).then_inc(s["loaded"], 16)
                        sp.dma_start(g2[:, :], p["g2"]).then_inc(s["loaded"], 16)
                        sp.dma_start(gng[:, :], row_broadcast(gn_g_row)).then_inc(s["loaded"], 16)
                        sp.dma_start(gnb[:, :], row_broadcast(gn_b_row)).then_inc(s["loaded"], 16)
                        sp.wait_ge(s["loaded"], 64)

                    @block.tensor
                    def _(pe):
                        pe.wait_ge(s["loaded"], 64)
                        pe.wait_ge(s["mixed"], DK)
                        accumulate(nc, low[:, :], [(g1[:, kk, :], mix[:, kk, :]) for kk in range(DK)]).then_inc(s["low_made"], 1)
                        pe.wait_ge(s["sg_done"], 1)
                        for tt in range(TT):
                            if tt:
                                pe.wait_ge(s["gate_taken"], tt)
                            for half in range(2):
                                last = nc.tensor.matmul(gate[:, half, :], sg[:, tt * P:(tt + 1) * P], g2[:, half * BANK:(half + 1) * BANK],
                                                        start=True, stop=True)
                            last.then_inc(s["gate_made"], 1)
                            pe.wait_ge(s["y_done"], tt + 1)
                            if tt:
                                pe.wait_ge(s["turn_taken"], tt)
                            for d in range(DK):
                                last = nc.tensor.transpose(turned[:, d // 4, (d % 4) * P:(d % 4 + 1) * P], y[:, tt, d * P:(d + 1) * P], k.ident[:, :])
                            last.then_inc(s["turn_made"], 1)

                    @block.scalar
                    def _(act):
                        act.wait_ge(s["low_made"], 1)
                        act.activation(sg[:, :], low[:, :], ACT.Sigmoid).then_inc(s["sg_done"], 1)
                        act.wait_ge(s["var_done"], 1)
                        act.activation(var[:, :], var[:, :], ACT.Sqrt).then_inc(s["root_done"], 1)
                        for tt in range(TT):
                            act.wait_ge(s["turn_made"], tt + 1)
                            for half in range(2):
                                last = act.activation(bh[:, half * 4:half * 4 + 4, tt * P:(tt + 1) * P],
                                                      turned[:, half, :].rearrange("p (d t) -> p d t", d=4), ACT.Copy)
                            last.then_inc(s["turn_taken"], 1)

                    @block.vector
                    def _(dve):
                        for j in range(DK):
                            nc.vector.tensor_tensor(diff[:, j % 2, :], k.ut[:, j, 0:T], k.ut[:, j, 1:T + 1], ALU.subtract).then_inc(s["diff_done"], 1)
                            dve.wait_ge(s["diff_done"], j + 1)
                            nc.vector.scalar_tensor_tensor(mix[:, j, :], diff[:, j % 2, :], k.cola[:, A_MU + 5 * DK + j:A_MU + 5 * DK + j + 1],
                                                           k.ut[:, j, 1:T + 1], ALU.mult, ALU.add).then_inc(s["mixed"], 1)
                        step = Chain(dve, s["dve_step"])
                        dve.wait_ge(s["loaded"], 64)
                        ya, va = (b_[:, :, :].rearrange("p t n -> p (t n)") for b_ in (y, v))
                        rows = lambda ap: ap.rearrange("p (a n) -> p a n", a=1).to_broadcast([P, TT, D])
                        step(nc.vector.tensor_reduce(mean[:, :], hv(ya), AX.X, ALU.add))
                        step(nc.vector.tensor_scalar(mean[:, :], mean[:, :], 1.0 / HD, None, ALU.mult))
                        step(nc.vector.tensor_tensor(hv(ya), hv(ya), bc(mean[:, :]), ALU.subtract))
                        step(nc.vector.tensor_tensor(tmp, ya, ya, ALU.mult))
                        step(nc.vector.tensor_reduce(var[:, :], hv(tmp), AX.X, ALU.add))
                        nc.vector.tensor_scalar(var[:, :], var[:, :], 1.0 / HD, RWKV_GN_EPS, ALU.mult, ALU.add).then_inc(s["var_done"], 1)
                        step(nc.vector.tensor_tensor(hv(tmp), hv(va), bc(bonus[:, :, :].rearrange("p t h -> p (t h)")), ALU.mult))
                        dve.wait_ge(s["root_done"], 1)
                        step(nc.vector.reciprocal(var[:, :], var[:, :]))
                        step(nc.vector.tensor_tensor(hv(ya), hv(ya), bc(var[:, :]), ALU.mult))
                        step(nc.vector.tensor_tensor(y[:, :, :], y[:, :, :], rows(gng[:, :]), ALU.mult))
                        step(nc.vector.tensor_tensor(y[:, :, :], y[:, :, :], rows(gnb[:, :]), ALU.add))
                        step(nc.vector.tensor_tensor(ya, ya, tmp, ALU.add))
                        for tt in range(TT):
                            yt = y[:, tt, :]
                            dve.wait_ge(s["gate_made"], tt + 1)
                            step(nc.vector.tensor_tensor(yt[:, 0:BANK], yt[:, 0:BANK], gate[:, 0, :], ALU.mult))
                            step(nc.vector.tensor_tensor(yt[:, BANK:D], yt[:, BANK:D], gate[:, 1, :], ALU.mult))
                            dve.sem_inc(s["gate_taken"], 1)
                            dve.sem_inc(s["y_done"], 1)
        project_norm_stage(nc, k, "rwkv_norm", bh, DK, p["w_out"], ga_row, ln_g, ln_b)


def conv_projection_stage(nc, k, name, w_in, col0, n_tiles, dst, taps, tok_w, tok_dst, small_w, small_dst, bias=None):
    CW, RING = 256, 3
    chunks = [w_in[:, col0 + c * CW:col0 + (c + 1) * CW] for c in range(n_tiles * P // CW)]
    n_feat = n_tiles
    tok_cols = tok_w.shape[1]
    chunks += [tok_w[:, c * CW:(c + 1) * CW] for c in range(tok_cols // CW)]
    n_groups = 2 * len(chunks)
    NS = small_w.shape[1]
    with Stage(nc, name) as st:
        ring = st.sb("ring", [P, RING, DK, CW])
        raw = st.sb("raw", [P, 2, T + CONV - 1])
        conv = st.sb("conv", [P, 2, T])
        small = st.sb("small", [P, DK, NS])
        ps = st.ps("ps", [P, 7, BANK])
        pss = st.ps("pss", [P, TT, NS])
        loaded = [st.sem(f"loaded{i}") for i in range(RING)]
        small_in, made, raw_done, conv_done, silu_done, tok_taken, zeroed, dstep, small_made, small_taken = (
            st.sem(n) for n in ("small_in", "made", "raw_done", "conv_done", "silu_done", "tok_taken", "zeroed", "dve_step",
                                "small_made", "small_taken"))
        with nc.Block() as block:
            @block.sync
            def _(sp):
                sp.dma_start(small[:, :, :], small_w.rearrange("(k p) n -> p k n", p=P)).then_inc(small_in, 16)
                for n, w in enumerate(chunks):
                    if n >= RING:
                        sp.wait_ge(made, 2 * (n - RING + 1))
                    sp.dma_start(ring[:, n % RING, :, :], w.rearrange("(k p) n -> p k n", p=P)).then_inc(loaded[n % RING], 16)

            @block.tensor
            def _(pe):
                for g in range(n_groups):
                    c = g // 2
                    if g >= 7:
                        before = g - 7
                        if before < n_feat:
                            pe.wait_ge(raw_done, before + 1)
                        else:
                            pe.wait_ge(tok_taken, before - n_feat + 1)
                    if g % 2 == 0:
                        pe.wait_ge(loaded[c % RING], 16 * (c // RING + 1))
                    if g < n_feat:
                        last = accumulate(nc, ps[:, g % 7, :], [(ring[:, c % RING, kk, (g % 2) * P:(g % 2 + 1) * P], k.ut[:, kk, 1:T + 1])
                                                                for kk in range(DK)])
                    else:
                        for q in range(2):
                            tt = (g % 2) * 2 + q
                            last = accumulate(nc, ps[:, g % 7, q * CW:(q + 1) * CW],
                                              [(k.ut[:, kk, 1 + tt * P:1 + (tt + 1) * P], ring[:, c % RING, kk, :]) for kk in range(DK)])
                    last.then_inc(made, 1)
                pe.wait_ge(small_in, 16)
                for tt in range(TT):
                    last = accumulate(nc, pss[:, tt, :], [(k.ut[:, kk, 1 + tt * P:1 + (tt + 1) * P], small[:, kk, :]) for kk in range(DK)])
                last.then_inc(small_made, 1)

            @block.scalar
            def _(act):
                act.wait_ge(zeroed, 1)
                def silu(g):
                    act.wait_ge(conv_done, g + 1)
                    act.activation(dst[:, g, :], conv[:, g % 2, :], ACT.Silu,
                                   bias=0.0 if bias is None else bias[:, g:g + 1]).then_inc(silu_done, 1)

                for g in range(n_feat):
                    act.wait_ge(made, g + 1)
                    if g >= 2:
                        act.wait_ge(conv_done, g - 1)
                    act.activation(raw[:, g % 2, CONV - 1:], ps[:, g % 7, :], ACT.Copy).then_inc(raw_done, 1)
                    if g:
                        silu(g - 1)
                silu(n_feat - 1)
                for g in range(n_feat, n_groups):
                    c, q = (g - n_feat) // 2, g % 2
                    act.wait_ge(made, g + 1)
                    act.activation(tok_dst[:, 2 * q:2 * q + 2, c * CW:(c + 1) * CW], ps[:, g % 7, :].rearrange("p (a n) -> p a n", a=2),
                                   ACT.Silu).then_inc(tok_taken, 1)

            @block.vector
            def _(dve):
                nc.vector.memset(raw[:, :, 0:CONV - 1], 0.0).then_inc(zeroed, 1)
                step = Chain(dve, dstep)
                for g in range(n_feat):
                    dve.wait_ge(raw_done, g + 1)
                    if g >= 2:
                        dve.wait_ge(silu_done, g - 1)
                    out = conv[:, g % 2, :]
                    for tap in range(CONV):
                        w = taps[:, tap * n_tiles + g:tap * n_tiles + g + 1]
                        src = raw[:, g % 2, tap:tap + T]
                        if tap == 0:
                            step(nc.vector.tensor_scalar(out, src, w, None, ALU.mult))
                        elif tap < CONV - 1:
                            step(nc.vector.scalar_tensor_tensor(out, src, w, out, ALU.mult, ALU.add))
                        else:
                            nc.vector.scalar_tensor_tensor(out, src, w, out, ALU.mult, ALU.add).then_inc(conv_done, 1)
                dve.wait_ge(small_made, 1)
                nc.vector.tensor_copy(small_dst[:, :, :], pss[:, :, :]).then_inc(small_taken, 1)
                dve.wait_ge(small_taken, 1)


class Softplus:

    def __init__(self, st, name, shape):
        self.e = st.sb(f"{name}_e", shape)
        self.abs_done, self.ln_done, self.mid = st.sem("abs_done"), st.sem("ln_done"), st.sem("exp_mid")

    def vector(self, nc, dve, step, x):
        nc.vector.scalar_tensor_tensor(self.e[:, :, :], x, -1.0, x, ALU.mult, ALU.max).then_inc(self.abs_done, 1)
        dve.wait_ge(self.ln_done, 1)
        step(nc.vector.tensor_scalar(x, x, 0.0, None, ALU.max))
        step(nc.vector.tensor_tensor(x, x, self.e[:, :, :], ALU.add))

    def scalar(self, act):
        act.wait_ge(self.abs_done, 1)
        act.activation(self.e[:, :, :], self.e[:, :, :], ACT.Exp, scale=-1.0).then_inc(self.mid, 1)
        act.wait_ge(self.mid, 1)
        act.activation(self.e[:, :, :], self.e[:, :, :], ACT.Ln, bias=1.0).then_inc(self.ln_done, 1)


def transpose_stage(nc, k, name, jobs):
    with Stage(nc, name) as st:
        ps = st.ps("ps", [P, 4, BANK])
        made, taken_a, taken_d = st.sem("made"), st.sem("taken_by_act"), st.sem("taken_by_dve")
        with nc.Block() as block:
            @block.tensor
            def _(pe):
                for n, (srcs, _) in enumerate(jobs):
                    if n >= 4:
                        pe.wait_ge((taken_a, taken_d)[n % 2], (n - 4) // 2 + 1)
                    for q in range(4):
                        last = nc.tensor.transpose(ps[:, n % 4, q * P:(q + 1) * P], srcs[q], k.ident[:, :])
                    last.then_inc(made, 1)

            @block.scalar
            def _(act):
                for n in range(0, len(jobs), 2):
                    act.wait_ge(made, n + 1)
                    act.activation(jobs[n][1], ps[:, n % 4, :].rearrange("p (a t) -> p a t", a=4), ACT.Copy).then_inc(taken_a, 1)

            @block.vector
            def _(dve):
                for n in range(1, len(jobs), 2):
                    dve.wait_ge(made, n + 1)
                    nc.vector.tensor_copy(jobs[n][1], ps[:, n % 4, :].rearrange("p (a t) -> p a t", a=4)).then_inc(taken_d, 1)


def gdn_stages(nc, k, a, ga_row, ln_g, ln_b):
    H, HW = GDN_HEADS, P
    w_in = a["gdn_w_in"][0]
    with Stage(nc, "gdn") as outer:
        kq = outer.sb("kq", [P, H, 2, T])
        v, z = outer.sb("v", [P, TT, D]), outer.sb("z", [P, TT, D])
        ba = outer.sb("ba", [P, TT, 2 * H])
        beta, g = outer.sb("beta", [P, TT, H]), outer.sb("g", [P, TT, H])
        gc, e_gc, e_rest, e_last = (outer.sb(n, [P, TT, H]) for n in ("gc", "e_gc", "e_rest", "e_last"))
        with Stage(nc, "gdn_flat") as fl:
            feat = fl.sb("feat", [P, QKV_TILES, T])
            conv_projection_stage(nc, k, "gdn_proj", w_in, 0, QKV_TILES, feat, k.colb, w_in[:, 3 * D:4 * D], z,
                                  w_in[:, 4 * D:4 * D + 2 * H], ba)
            transpose_stage(nc, k, "gdn_turn_v", [([feat[:, 2 * H + half * 4 + q, tt * P:(tt + 1) * P] for q in range(4)],
                                                   v[:, tt, half * BANK:(half + 1) * BANK].rearrange("p (a t) -> p a t", a=4))
                                                  for tt in range(TT) for half in range(2)])
            with Stage(nc, "gdn_norm") as st:
                inv = st.sb("inv", [P, 2, T])
                sq = st.sb("sq", [P, 2, T])
                dt_row, alog_row = st.sb("dt_row", [P, H]), st.sb("alog_row", [P, H])
                sp_ = Softplus(st, "softplus", [P, TT, H])
                norm, sums = st.ps("norm", [P, 2, BANK]), st.ps("sums", [P, 2, TT, H])
                names = ("rows_in", "sq_done", "norm_done", "eps_done", "root_done", "dve_step", "beta_done", "alog_done", "g_done",
                         "sums_done", "arg_done", "exp_done")
                s = {n: st.sem(n) for n in names}
                with nc.Block() as block:
                    @block.sync
                    def _(sp):
                        sp.dma_start(dt_row[:, :], row_broadcast(a["gdn_dt_bias"][0])).then_inc(s["rows_in"], 16)
                        sp.dma_start(alog_row[:, :], row_broadcast(a["gdn_a_log"][0])).then_inc(s["rows_in"], 16)
                        sp.wait_ge(s["rows_in"], 32)

                    @block.vector
                    def _(dve):
                        step = Chain(dve, s["dve_step"])
                        dve.wait_ge(s["rows_in"], 32)
                        step(nc.vector.tensor_tensor(g[:, :, :], ba[:, :, H:2 * H], dt_row[:, :].rearrange("p (a h) -> p a h", a=1).to_broadcast([P, TT, H]), ALU.add))
                        sp_.vector(nc, dve, step, g[:, :, :])
                        dve.wait_ge(s["alog_done"], 1)
                        nc.vector.scalar_tensor_tensor(g[:, :, :], g[:, :, :], -1.0,
                                                       alog_row[:, :].rearrange("p (a h) -> p a h", a=1).to_broadcast([P, TT, H]),
                                                       ALU.mult, ALU.mult).then_inc(s["g_done"], 1)
                        dve.wait_ge(s["sums_done"], 1)
                        step(nc.vector.tensor_copy(gc[:, :, :], sums[:, 0, :, :]))
                        step(nc.vector.tensor_copy(e_last[:, :, :], sums[:, 1, :, :]))
                        nc.vector.tensor_tensor(e_rest[:, :, :], e_last[:, :, :], gc[:, :, :], ALU.subtract).then_inc(s["arg_done"], 1)
                        for n in range(2 * H):
                            side, h = n // H, n % H
                            if n >= 1:
                                dve.wait_ge(s["norm_done"], n)
                            step(nc.vector.tensor_tensor(sq[:, n % 2, :], feat[:, n, :], feat[:, n, :], ALU.mult))
                            dve.sem_inc(s["sq_done"], 1)
                            dve.wait_ge(s["norm_done"], n + 1)
                            nc.vector.tensor_scalar(inv[:, n % 2, :], norm[:, n % 2, :], 1e-6, None, ALU.add).then_inc(s["eps_done"], 1)
                            dve.wait_ge(s["root_done"], n + 1)
                            step(nc.vector.reciprocal(inv[:, n % 2, :], inv[:, n % 2, :]))
                            step(nc.vector.scalar_tensor_tensor(kq[:, h, 1 - side, :], feat[:, n, :], (P ** -0.5, 1.0)[side], inv[:, n % 2, :],
                                                                ALU.mult, ALU.mult))

                    @block.tensor
                    def _(pe):
                        pe.wait_ge(s["g_done"], 1)
                        for tt in range(TT):
                            nc.tensor.matmul(sums[:, 0, tt, :], k.causal[:, 1, :], g[:, tt, :], start=True, stop=True)
                            last = nc.tensor.matmul(sums[:, 1, tt, :], k.ones[:, :], g[:, tt, :], start=True, stop=True)
                        last.then_inc(s["sums_done"], 1)
                        for n in range(2 * H):
                            pe.wait_ge(s["sq_done"], n + 1)
                            nc.tensor.matmul(norm[:, n % 2, :], k.ones[:, :], sq[:, n % 2, :], start=True, stop=True).then_inc(s["norm_done"], 1)

                    @block.scalar
                    def _(act):
                        act.activation(beta[:, :, :], ba[:, :, 0:H], ACT.Sigmoid).then_inc(s["beta_done"], 1)
                        act.wait_ge(s["rows_in"], 32)
                        act.activation(alog_row[:, :], alog_row[:, :], ACT.Exp).then_inc(s["alog_done"], 1)
                        sp_.scalar(act)
                        act.wait_ge(s["arg_done"], 1)
                        act.activation(e_gc[:, :, :], gc[:, :, :], ACT.Exp)
                        act.activation(e_rest[:, :, :], e_rest[:, :, :], ACT.Exp)
                        act.activation(e_last[:, :, :], e_last[:, :, :], ACT.Exp).then_inc(s["exp_done"], 1)
                        act.wait_ge(s["exp_done"], 1)
                        for n in range(2 * H):
                            act.wait_ge(s["eps_done"], n + 1)
                            act.activation(inv[:, n % 2, :], inv[:, n % 2, :], ACT.Sqrt).then_inc(s["root_done"], 1)

        with Stage(nc, "gdn_rec") as rec:
            ITEMS = NC * 2
            lt, at = rec.sb("lt", [P, ITEMS, 4 * P]), rec.sb("at", [P, ITEMS, 4 * P])
            y = rec.sb("y", [P, TT, D])
            with Stage(nc, "gdn_low") as st:
                dec = st.sb("dec", [P, 2, 4, P])
                dmask = st.sb("dmask", [P, 2, 2, 4, P])
                ps = st.ps("ps", [P, 2, 4, BANK])
                names = ("made", "arg_done", "exp_done", "masked", "taken", "dve_step")
                s = {n: st.sem(n) for n in names}
                with nc.Block() as block:
                    @block.tensor
                    def _(pe):
                        for n in range(ITEMS):
                            c, b = n // 2, n % 2
                            if n >= 2:
                                pe.wait_ge(s["taken"], n - 1)
                            for q in range(4):
                                h = (n % 2) * 4 + q
                                nc.tensor.matmul(ps[:, b, 2, q * P:(q + 1) * P], g[:, c, h:h + 1].to_broadcast([P, P]), k.causal[:, 1, :], start=True, stop=True)
                                nc.tensor.matmul(ps[:, b, 3, q * P:(q + 1) * P], beta[:, c, h:h + 1].to_broadcast([P, P]), k.ident[:, :], start=True, stop=True)
                                last = nc.tensor.matmul(ps[:, b, q // 2, (q % 2) * 2 * P:(q % 2 + 1) * 2 * P], kq[:, h, 0, c * CH:(c + 1) * CH],
                                                        kq[:, h, :, c * CH:(c + 1) * CH], start=True, stop=True)
                            last.then_inc(s["made"], 1)

                    @block.scalar
                    def _(act):
                        for n in range(ITEMS):
                            act.wait_ge(s["arg_done"], n + 1)
                            act.activation(dec[:, n % 2, :, :], dec[:, n % 2, :, :], ACT.Exp).then_inc(s["exp_done"], 1)

                    @block.gpsimd
                    def _(pool):
                        for n in range(ITEMS):
                            pool.wait_ge(s["exp_done"], n + 1)
                            if n >= 2:
                                pool.wait_ge(s["taken"], n - 1)
                            for m in range(2):
                                last = nc.gpsimd.tensor_tensor(dmask[:, n % 2, m, :, :], dec[:, n % 2, :, :],
                                                               k.causal[:, m:m + 1, :].to_broadcast([P, 4, P]), ALU.mult)
                            last.then_inc(s["masked"], 1)

                    @block.vector
                    def _(dve):
                        step = Chain(dve, s["dve_step"])
                        for n in range(ITEMS):
                            c, b = n // 2, n % 2
                            dve.wait_ge(s["made"], n + 1)
                            if n >= 2:
                                dve.wait_ge(s["masked"], n - 1)
                            for q in range(4):
                                h = (n % 2) * 4 + q
                                last = nc.vector.tensor_scalar(dec[:, b, q, :], ps[:, b, 2, q * P:(q + 1) * P], gc[:, c, h:h + 1], 0.0, ALU.subtract, ALU.min)
                            last.then_inc(s["arg_done"], 1)
                            dve.wait_ge(s["masked"], n + 1)
                            for half in range(2):
                                pv = ps[:, b, half, :].rearrange("p (q w t) -> p q w t", q=2, w=2)
                                lv = lt[:, n, half * 2 * P:(half + 1) * 2 * P].rearrange("p (q t) -> p q t", q=2)
                                av = at[:, n, half * 2 * P:(half + 1) * 2 * P].rearrange("p (q t) -> p q t", q=2)
                                step(nc.vector.scalar_tensor_tensor(lv, pv[:, :, 0, :], -1.0, dmask[:, b, 0, half * 2:half * 2 + 2, :], ALU.mult, ALU.mult))
                                step(nc.vector.tensor_tensor(av, pv[:, :, 1, :], dmask[:, b, 1, half * 2:half * 2 + 2, :], ALU.mult))
                            nc.vector.tensor_tensor(lt[:, n, :], lt[:, n, :], ps[:, b, 3, :], ALU.mult).then_inc(s["taken"], 1)
            inverse_stage(nc, k, "gdn_inv", lt, ITEMS)
            with Stage(nc, "gdn_scan") as st:
                state = st.sb("state", [P, H, HW])
                tok = st.sb("tok", [P, 2, 4, P])
                rhs, u, qs = (st.sb(n, [P, 2, 4, P]) for n in ("rhs", "u", "qs"))
                ps = st.ps("ps", [P, 6, 4, P])
                names = ("zeroed", "tok_made", "tok_taken", "ks_made", "rhs_done", "qs_taken", "u_made", "u_taken", "y_made", "y_done",
                         "s_made", "s_done", "dve_step")
                s = {n: st.sem(n) for n in names}
                with nc.Block() as block:
                    @block.gpsimd
                    def _(pool):
                        nc.gpsimd.memset(state[:, :, :], 0.0).then_inc(s["zeroed"], 1)

                    @block.tensor
                    def _(pe):
                        pe.wait_ge(s["zeroed"], 1)
                        for n in range(ITEMS):
                            c, b, h0 = n // 2, n % 2, (n % 2) * 4
                            t = slice(c * CH, (c + 1) * CH)
                            if n:
                                pe.wait_ge(s["tok_taken"], n)
                            for q in range(4):
                                last = nc.tensor.transpose(ps[:, 5, q, :], kq[:, h0 + q, 0, t], k.ident[:, :])
                            last.then_inc(s["tok_made"], 1)
                            if n:
                                pe.wait_ge(s["rhs_done"], n)
                                pe.wait_ge(s["qs_taken"], n)
                            if n >= 2:
                                pe.wait_ge(s["s_done"], n - 1)
                            for q in range(4):
                                nc.tensor.matmul(ps[:, 0, q, :], kq[:, h0 + q, 0, t], state[:, h0 + q, :], start=True, stop=True)
                            for q in range(4):
                                last = nc.tensor.matmul(ps[:, 1, q, :], kq[:, h0 + q, 1, t], state[:, h0 + q, :], start=True, stop=True)
                            last.then_inc(s["ks_made"], 1)
                            pe.wait_ge(s["rhs_done"], n + 1)
                            for q in range(4):
                                last = nc.tensor.matmul(ps[:, 2, q, :], lt[:, n, q * P:(q + 1) * P], rhs[:, b, q, :], start=True, stop=True)
                            last.then_inc(s["u_made"], 1)
                            pe.wait_ge(s["u_taken"], n + 1)
                            if n:
                                pe.wait_ge(s["y_done"], n)
                            for q in range(4):
                                last = nc.tensor.matmul(ps[:, 3, q, :], at[:, n, q * P:(q + 1) * P], u[:, b, q, :], start=True, stop=True)
                            last.then_inc(s["y_made"], 1)
                            pe.wait_ge(s["tok_taken"], n + 1)
                            if n:
                                pe.wait_ge(s["s_done"], n)
                            for q in range(4):
                                last = nc.tensor.matmul(ps[:, 4, q, :], tok[:, b, q, :], u[:, b, q, :], start=True, stop=True)
                            last.then_inc(s["s_made"], 1)

                    @block.scalar
                    def _(act):
                        for n in range(ITEMS):
                            c, b, h0 = n // 2, n % 2, (n % 2) * 4
                            act.wait_ge(s["tok_made"], n + 1)
                            if n >= 2:
                                act.wait_ge(s["s_made"], n - 1)
                            for q in range(4):
                                last = act.activation(tok[:, b, q, :], ps[:, 5, q, :], ACT.Copy, scale=e_rest[:, c, h0 + q:h0 + q + 1])
                            last.then_inc(s["tok_taken"], 1)
                            act.wait_ge(s["ks_made"], n + 1)
                            if n >= 2:
                                act.wait_ge(s["y_done"], n - 1)
                            for q in range(4):
                                last = act.activation(qs[:, b, q, :], ps[:, 1, q, :], ACT.Copy, scale=e_gc[:, c, h0 + q:h0 + q + 1])
                            last.then_inc(s["qs_taken"], 1)
                            act.wait_ge(s["u_made"], n + 1)
                            act.activation(u[:, b, :, :], ps[:, 2, :, :], ACT.Copy).then_inc(s["u_taken"], 1)

                    @block.vector
                    def _(dve):
                        step = Chain(dve, s["dve_step"])
                        for n in range(ITEMS):
                            c, b, h0 = n // 2, n % 2, (n % 2) * 4
                            sc = lambda t_: t_[:, c, h0:h0 + 4].unsqueeze(2).to_broadcast([P, 4, P])
                            dve.wait_ge(s["ks_made"], n + 1)
                            r = rhs[:, b, :, :]
                            step(nc.vector.tensor_tensor(r, ps[:, 0, :, :], sc(e_gc), ALU.mult))
                            step(nc.vector.tensor_tensor(r, v[:, c, h0 * P:(h0 + 4) * P].rearrange("p (q n) -> p q n", q=4), r, ALU.subtract))
                            nc.vector.tensor_tensor(r, r, sc(beta), ALU.mult).then_inc(s["rhs_done"], 1)
                            dve.wait_ge(s["y_made"], n + 1)
                            dve.wait_ge(s["qs_taken"], n + 1)
                            nc.vector.tensor_tensor(y[:, c, h0 * P:(h0 + 4) * P].rearrange("p (q n) -> p q n", q=4), ps[:, 3, :, :],
                                                    qs[:, b, :, :], ALU.add).then_inc(s["y_done"], 1)
                            dve.wait_ge(s["s_made"], n + 1)
                            sl = state[:, h0:h0 + 4, :]
                            step(nc.vector.tensor_tensor(sl, sl, sc(e_last), ALU.mult))
                            nc.vector.tensor_tensor(sl, sl, ps[:, 4, :, :], ALU.add).then_inc(s["s_done"], 1)
            yt = kq[:, :, :, :].rearrange("p h w t -> p (h w t)")[:, 0:DK * T].rearrange("p (d t) -> p d t", d=DK)
            rms_gate_stage(nc, k, "gdn_out", y, z, TT * H, HW, 1e-6, a["gdn_norm_g"][0], at)
            transpose_stage(nc, k, "gdn_turn_y", [([y[:, tt, (half * 4 + q) * P:(half * 4 + q + 1) * P] for q in range(4)],
                                                   yt[:, half * 4:half * 4 + 4, tt * P:(tt + 1) * P])
                                                  for tt in range(TT) for half in range(2)])
            project_norm_stage(nc, k, "gdn_norm2", yt, DK, a["gdn_w_out"][0], ga_row, ln_g, ln_b)


def rms_gate_stage(nc, k, name, y, z, groups, width, eps, g_row, tmp):
    with Stage(nc, name) as st:
        ss = st.sb("ss", [P, groups])
        n_g = g_row.shape[0]
        gr = st.sb("gr", [P, n_g])
        rows_in, var_done, root_done, dstep = st.sem("rows_in"), st.sem("var_done"), st.sem("root_done"), st.sem("dve_step")
        flat = lambda b: b.rearrange("p t n -> p (t n)")
        hv = lambda ap: ap.rearrange("p (h n) -> p h n", h=groups)
        ya = flat(y[:, :, :])
        ta = flat(tmp[:, :, :])
        with nc.Block() as block:
            @block.sync
            def _(sp):
                sp.dma_start(gr[:, :], row_broadcast(g_row)).then_inc(rows_in, 16)
                sp.wait_ge(rows_in, 16)

            @block.scalar
            def _(act):
                act.wait_ge(var_done, 1)
                act.activation(ss[:, :], ss[:, :], ACT.Sqrt).then_inc(root_done, 1)

            @block.vector
            def _(dve):
                step = Chain(dve, dstep)
                step(nc.vector.tensor_tensor(ta, ya, ya, ALU.mult))
                step(nc.vector.tensor_reduce(ss[:, :], hv(ta), AX.X, ALU.add))
                nc.vector.tensor_scalar(ss[:, :], ss[:, :], 1.0 / width, eps, ALU.mult, ALU.add).then_inc(var_done, 1)
                if z is not None:
                    step(nc.vector.tensor_tensor(ya, ya, flat(z[:, :, :]), ALU.mult))
                dve.wait_ge(rows_in, 16)
                reps = ya.shape[1] // n_g
                step(nc.vector.tensor_tensor(ya.rearrange("p (r n) -> p r n", r=reps), ya.rearrange("p (r n) -> p r n", r=reps),
                                             gr[:, :].rearrange("p (r n) -> p r n", r=1).to_broadcast([P, reps, n_g]), ALU.mult))
                dve.wait_ge(root_done, 1)
                step(nc.vector.reciprocal(ss[:, :], ss[:, :]))
                step(nc.vector.tensor_tensor(hv(ya), hv(ya), ss[:, :].unsqueeze(2).to_broadcast([P, groups, width]), ALU.mult))


SSD_HEADS, SSD_GROUPS, SSD_INNER = 32, 4, 2048
SSD_EPS = 1e-5


def ssd_stages(nc, k, a, ln_g, ln_b):
    H, G, E, N = SSD_HEADS, SSD_GROUPS, SSD_HEADS // SSD_GROUPS, P
    w_in = a["ssd_w_in_2"][0]
    XBC = SSD_INNER
    with Stage(nc, "ssd") as outer:
        feat = outer.sb("feat", [P, SSD_TILES, T])
        z = outer.sb("z", [P, TT, SSD_INNER])
        dt, cs, e_cs, e_rest, e_last = (outer.sb(n, [P, TT, H]) for n in ("dt", "cs", "e_cs", "e_rest", "e_last"))
        da = outer.sb("da", [P, TT, H])
        d_row = outer.sb("d_row", [P, H])
        conv_projection_stage(nc, k, "ssd_proj", w_in, XBC, SSD_TILES, feat, k.colc, w_in[:, 0:SSD_INNER], z,
                              w_in[:, XBC + SSD_TILES * P:], dt, bias=k.colc[:, CONV * SSD_TILES:5 * SSD_TILES])
        with Stage(nc, "ssd_rec") as rec:
            xs = rec.sb("xs", [P, TT, SSD_INNER])
            bt = rec.sb("bt", [P, TT, G * N])
            jobs = [([feat[:, m * 4 + q, tt * P:(tt + 1) * P] for q in range(4)],
                     (xs[:, tt, m * BANK:(m + 1) * BANK] if m < 4 else bt[:, tt, :]).rearrange("p (a t) -> p a t", a=4))
                    for tt in range(TT) for m in range(5)]
            transpose_stage(nc, k, "ssd_turn_x", jobs)
            with Stage(nc, "ssd_steps") as st:
                dt_row, alog_row = st.sb("dt_row", [P, H]), st.sb("alog_row", [P, H])
                sp_ = Softplus(st, "softplus", [P, TT, H])
                sums = st.ps("sums", [P, 2, TT, H])
                s = {n: st.sem(n) for n in ("rows_in", "dve_step", "alog_done", "da_done", "sums_done", "arg_done", "exp_done")}
                rows = lambda r: r[:, :].rearrange("p (a h) -> p a h", a=1).to_broadcast([P, TT, H])
                with nc.Block() as block:
                    @block.sync
                    def _(sp):
                        sp.dma_start(dt_row[:, :], row_broadcast(a["ssd_dt_bias_2"][0])).then_inc(s["rows_in"], 16)
                        sp.dma_start(alog_row[:, :], row_broadcast(a["ssd_a_log_2"][0])).then_inc(s["rows_in"], 16)
                        sp.dma_start(d_row[:, :], row_broadcast(a["ssd_d_2"][0])).then_inc(s["rows_in"], 16)
                        sp.wait_ge(s["rows_in"], 48)

                    @block.vector
                    def _(dve):
                        step = Chain(dve, s["dve_step"])
                        dve.wait_ge(s["rows_in"], 48)
                        step(nc.vector.tensor_tensor(dt[:, :, :], dt[:, :, :], rows(dt_row), ALU.add))
                        sp_.vector(nc, dve, step, dt[:, :, :])
                        dve.wait_ge(s["alog_done"], 1)
                        nc.vector.scalar_tensor_tensor(da[:, :, :], dt[:, :, :], -1.0, rows(alog_row), ALU.mult, ALU.mult).then_inc(s["da_done"], 1)
                        dve.wait_ge(s["sums_done"], 1)
                        step(nc.vector.tensor_copy(cs[:, :, :], sums[:, 0, :, :]))
                        step(nc.vector.tensor_copy(e_last[:, :, :], sums[:, 1, :, :]))
                        nc.vector.tensor_tensor(e_rest[:, :, :], e_last[:, :, :], cs[:, :, :], ALU.subtract).then_inc(s["arg_done"], 1)

                    @block.tensor
                    def _(pe):
                        pe.wait_ge(s["da_done"], 1)
                        for tt in range(TT):
                            nc.tensor.matmul(sums[:, 0, tt, :], k.causal[:, 1, :], da[:, tt, :], start=True, stop=True)
                            last = nc.tensor.matmul(sums[:, 1, tt, :], k.ones[:, :], da[:, tt, :], start=True, stop=True)
                        last.then_inc(s["sums_done"], 1)

                    @block.scalar
                    def _(act):
                        act.wait_ge(s["rows_in"], 48)
                        act.activation(alog_row[:, :], alog_row[:, :], ACT.Exp).then_inc(s["alog_done"], 1)
                        sp_.scalar(act)
                        act.wait_ge(s["arg_done"], 1)
                        act.activation(e_cs[:, :, :], cs[:, :, :], ACT.Exp)
                        act.activation(e_rest[:, :, :], e_rest[:, :, :], ACT.Exp)
                        act.activation(e_last[:, :, :], e_last[:, :, :], ACT.Exp).then_inc(s["exp_done"], 1)
            with Stage(nc, "ssd_scan") as st:
                HP = 64
                GW = E * HP
                state = st.sb("state", [P, G, GW])
                xdt, xrest, xd = (st.sb(n, [P, 2, E, HP]) for n in ("xdt", "xrest", "xd"))
                dec, m = st.sb("dec", [P, 2, E, P]), st.sb("m", [P, E, P])
                yv = st.sb("yv", [P, GW])
                ps = st.ps("ps", [P, 6, BANK])
                names = ("x_done", "gb_made", "arg_done", "exp_done", "masked", "cb_made", "m_done", "yd_made", "off_made", "y_done",
                         "s_made", "s_done", "zeroed", "dve_step")
                s = {n: st.sem(n) for n in names}
                e2 = lambda ap: ap.rearrange("p (e n) -> p e n", e=E)
                with nc.Block() as block:
                    @block.gpsimd
                    def _(pool):
                        nc.gpsimd.memset(state[:, :, :], 0.0).then_inc(s["zeroed"], 1)
                        for n in range(NC * G):
                            c, g, b = n // G, n % G, n % 2
                            sc = lambda t_, w: t_[:, c, g * E:(g + 1) * E].unsqueeze(2).to_broadcast([P, E, w])
                            x = e2(xs[:, c, g * GW:(g + 1) * GW])
                            if n >= 2:
                                pool.wait_ge(s["s_done"], n - 1)
                                pool.wait_ge(s["y_done"], n - 1)
                            nc.gpsimd.tensor_tensor(xd[:, b, :, :], x, d_row[:, g * E:(g + 1) * E].unsqueeze(2).to_broadcast([P, E, HP]), ALU.mult)
                            nc.gpsimd.tensor_tensor(xdt[:, b, :, :], x, sc(dt, HP), ALU.mult).then_inc(s["x_done"], 1)
                            pool.wait_ge(s["x_done"], 2 * n + 1)
                            nc.gpsimd.tensor_tensor(xrest[:, b, :, :], xdt[:, b, :, :], sc(e_rest, HP), ALU.mult).then_inc(s["x_done"], 1)
                            pool.wait_ge(s["exp_done"], n + 1)
                            nc.gpsimd.tensor_tensor(dec[:, b, :, :], dec[:, b, :, :], k.causal[:, 1:2, :].to_broadcast([P, E, P]), ALU.mult).then_inc(s["masked"], 1)

                    @block.tensor
                    def _(pe):
                        pe.wait_ge(s["zeroed"], 1)
                        for n in range(NC * G):
                            c, g, b = n // G, n % G, n % 2
                            t = slice(c * CH, (c + 1) * CH)
                            if n:
                                pe.wait_ge(s["arg_done"], n)
                            for e in range(E):
                                h = g * E + e
                                last = nc.tensor.matmul(ps[:, 1 + e // 4, (e % 4) * P:(e % 4 + 1) * P], da[:, c, h:h + 1].to_broadcast([P, P]),
                                                        k.causal[:, 1, :], start=True, stop=True)
                            last.then_inc(s["gb_made"], 1)
                            if n:
                                pe.wait_ge(s["m_done"], n)
                            nc.tensor.matmul(ps[:, 0, 0:P], feat[:, 16 + g, t], feat[:, 20 + g, t], start=True, stop=True).then_inc(s["cb_made"], 1)
                            if n:
                                pe.wait_ge(s["y_done"], n)
                            if n >= G:
                                pe.wait_ge(s["s_done"], n - G + 1)
                            nc.tensor.matmul(ps[:, 4, :], feat[:, 20 + g, t], state[:, g, :], start=True, stop=True).then_inc(s["off_made"], 1)
                            pe.wait_ge(s["x_done"], 2 * n + 2)
                            if n:
                                pe.wait_ge(s["s_done"], n)
                            nc.tensor.matmul(ps[:, 5, :], bt[:, c, g * N:(g + 1) * N], xrest[:, b, :, :], start=True, stop=True).then_inc(s["s_made"], 1)
                            pe.wait_ge(s["m_done"], n + 1)
                            for e in range(E):
                                last = nc.tensor.matmul(ps[:, 3, e * HP:(e + 1) * HP], m[:, e, :], xdt[:, b, e, :], start=True, stop=True)
                            last.then_inc(s["yd_made"], 1)

                    @block.scalar
                    def _(act):
                        for n in range(NC * G):
                            act.wait_ge(s["arg_done"], n + 1)
                            act.activation(dec[:, n % 2, :, :], dec[:, n % 2, :, :], ACT.Exp).then_inc(s["exp_done"], 1)

                    @block.vector
                    def _(dve):
                        step = Chain(dve, s["dve_step"])
                        dve.wait_ge(s["zeroed"], 1)
                        for n in range(NC * G):
                            c, g, b = n // G, n % G, n % 2
                            sc = lambda t_, w: t_[:, c, g * E:(g + 1) * E].unsqueeze(2).to_broadcast([P, E, w])
                            dve.wait_ge(s["gb_made"], n + 1)
                            for e in range(E):
                                h = g * E + e
                                last = nc.vector.tensor_scalar(dec[:, b, e, :], ps[:, 1 + e // 4, (e % 4) * P:(e % 4 + 1) * P], cs[:, c, h:h + 1], 0.0,
                                                               ALU.subtract, ALU.min)
                            last.then_inc(s["arg_done"], 1)
                            dve.wait_ge(s["masked"], n + 1)
                            dve.wait_ge(s["cb_made"], n + 1)
                            if n:
                                dve.wait_ge(s["yd_made"], n)
                            nc.vector.tensor_tensor(m[:, :, :], dec[:, b, :, :], ps[:, 0, 0:P].rearrange("p (a t) -> p a t", a=1).to_broadcast([P, E, P]),
                                                    ALU.mult).then_inc(s["m_done"], 1)
                            dve.wait_ge(s["s_made"], n + 1)
                            dve.wait_ge(s["off_made"], n + 1)
                            sl = e2(state[:, g, :])
                            step(nc.vector.tensor_tensor(sl, sl, sc(e_last, HP), ALU.mult))
                            nc.vector.tensor_tensor(state[:, g, :], state[:, g, :], ps[:, 5, :], ALU.add).then_inc(s["s_done"], 1)
                            step(nc.vector.tensor_tensor(e2(yv[:, :]), e2(ps[:, 4, :]), sc(e_cs, HP), ALU.mult))
                            step(nc.vector.tensor_tensor(e2(yv[:, :]), e2(yv[:, :]), xd[:, b, :, :], ALU.add))
                            dve.wait_ge(s["yd_made"], n + 1)
                            step(nc.vector.tensor_tensor(yv[:, :], yv[:, :], ps[:, 3, :], ALU.add))
                            zs = z[:, c, g * GW:(g + 1) * GW]
                            nc.vector.tensor_tensor(zs, zs, yv[:, :], ALU.mult).then_inc(s["y_done"], 1)
                            dve.wait_ge(s["y_done"], n + 1)
            rms_gate_stage(nc, k, "ssd_out", z, None, TT * G, SSD_INNER // G, SSD_EPS, a["ssd_norm_w_2"][0], xs)
        yt = feat[:, 0:16, :]
        transpose_stage(nc, k, "ssd_turn_y", [([z[:, tt, (m * 4 + q) * P:(m * 4 + q + 1) * P] for q in range(4)],
                                               yt[:, m * 4:m * 4 + 4, tt * P:(tt + 1) * P])
                                              for tt in range(TT) for m in range(4)])
        project_norm_stage(nc, k, "ssd_norm", yt, 16, a["ssd_w_out_2"][0], None, ln_g, ln_b)


ATT_HEADS, ATT_GROUPS, ATT_HD = 8, 3, 64
ROPE_HALF = 8
ROPE_THETA = 500000.0
STRIDE = 4
NEG = -1e30


def attention_stages(nc, k, a, ln_g, ln_b):
    R, G, H = STRIDE, ATT_GROUPS, ATT_HEADS
    HB = H * ATT_HD
    w_qkv = a["attn_w_qkv_2"][0]
    with Stage(nc, "att") as outer:
        kqt = outer.sb("kqt", [P, G, 2, 4, R, P])
        v = outer.sb("v", [P, R, G, HB])
        ot = outer.sb("ot", [P, 4, T])
        with Stage(nc, "att_tok") as tk:
            qk = tk.sb("qk", [P, R, G, 2, HB])
            cos, sin = tk.sb("cos", [P, R, ROPE_HALF]), tk.sb("sin", [P, R, ROPE_HALF])
            with Stage(nc, "att_rope") as st:
                pos_i, pos = st.sb("pos_i", [P, R], I32), st.sb("pos", [P, R])
                freq, ang, turns = st.sb("freq", [P, ROPE_HALF]), st.sb("ang", [P, R, ROPE_HALF]), st.sb("turns", [P, R, ROPE_HALF])
                loaded, dstep, ready, done = st.sem("loaded"), st.sem("dve_step"), st.sem("ready"), st.sem("done")
                TWO_PI = 2 * np.pi
                C1 = float(np.float32(6.28125))
                C2 = float(np.float32(np.round((TWO_PI - C1) * 2 ** 21) / 2 ** 21))
                C3 = float(np.float32(TWO_PI - C1 - C2))
                ROUND = 12582912.0
                LIM = 3.1415925
                with nc.Block() as block:
                    @block.sync
                    def _(sp):
                        sp.dma_start(pos_i[:, :], a["positions_2"][0].rearrange("(j r) -> j r", r=R)).then_inc(loaded, 16)
                        sp.wait_ge(loaded, 16)

                    @block.vector
                    def _(dve):
                        step = Chain(dve, dstep)
                        for i in range(ROPE_HALF):
                            f = float(np.float32(ROPE_THETA) ** np.float32(-(2.0 * i) / (2 * ROPE_HALF)))
                            step(nc.vector.memset(freq[:, i:i + 1], f))
                        dve.wait_ge(loaded, 16)
                        step(nc.vector.tensor_copy(pos[:, :], pos_i[:, :]))
                        step(nc.vector.tensor_tensor(ang[:, :, :], pos[:, :].unsqueeze(2).to_broadcast([P, R, ROPE_HALF]),
                                                     freq[:, :].rearrange("p (a i) -> p a i", a=1).to_broadcast([P, R, ROPE_HALF]), ALU.mult))
                        step(nc.vector.tensor_scalar(turns[:, :, :], ang[:, :, :], float(1 / TWO_PI), None, ALU.mult))
                        step(nc.vector.tensor_scalar(turns[:, :, :], turns[:, :, :], ROUND, None, ALU.add))
                        step(nc.vector.tensor_scalar(turns[:, :, :], turns[:, :, :], -ROUND, None, ALU.add))
                        for cst in (C1, C2, C3):
                            step(nc.vector.scalar_tensor_tensor(ang[:, :, :], turns[:, :, :], -cst, ang[:, :, :], ALU.mult, ALU.add))
                        step(nc.vector.tensor_scalar(sin[:, :, :], ang[:, :, :], LIM, -LIM, ALU.min, ALU.max))
                        step(nc.vector.tensor_scalar(ang[:, :, :], ang[:, :, :], float(np.pi / 2), None, ALU.add))
                        step(nc.vector.tensor_scalar(turns[:, :, :], ang[:, :, :], LIM, -TWO_PI, ALU.is_gt, ALU.mult))
                        step(nc.vector.tensor_tensor(ang[:, :, :], ang[:, :, :], turns[:, :, :], ALU.add))
                        nc.vector.tensor_scalar(cos[:, :, :], ang[:, :, :], LIM, -LIM, ALU.min, ALU.max).then_inc(ready, 1)

                    @block.scalar
                    def _(act):
                        act.wait_ge(ready, 1)
                        act.activation(sin[:, :, :], sin[:, :, :], ACT.Sin).then_inc(done, 1)
                        act.activation(cos[:, :, :], cos[:, :, :], ACT.Sin).then_inc(done, 1)
            with Stage(nc, "att_proj") as st:
                RING, CB = 2, 3 * G
                ring = st.sb("ring", [P, RING, DK, HB])
                t1, t2 = st.sb("t1", [P, 2, H, ROPE_HALF]), st.sb("t2", [P, 2, H, ROPE_HALF])
                ps = st.ps("ps", [P, 8, BANK])
                loaded = [st.sem(f"loaded{i}") for i in range(RING)]
                made, taken, dstep = st.sem("made"), st.sem("taken"), st.sem("dve_step")
                with nc.Block() as block:
                    @block.sync
                    def _(sp):
                        for n in range(CB):
                            if n >= RING:
                                sp.wait_ge(made, R * (n - RING + 1))
                            sp.dma_start(ring[:, n % RING, :, :], w_qkv[:, n * HB:(n + 1) * HB].rearrange("(k p) n -> p k n", p=P)).then_inc(loaded[n % RING], 16)

                    @block.tensor
                    def _(pe):
                        for n in range(CB):
                            pe.wait_ge(loaded[n % RING], 16 * (n // RING + 1))
                            for r in range(R):
                                g = n * R + r
                                if g >= 8:
                                    pe.wait_ge(taken, g - 7)
                                accumulate(nc, ps[:, g % 8, :], [(k.ut[:, kk, 1 + r:1 + T:R], ring[:, n % RING, kk, :]) for kk in range(DK)]).then_inc(made, 1)

                    @block.scalar
                    def _(act):
                        for n in range(CB):
                            for r in range(R):
                                g = n * R + r
                                act.wait_ge(made, g + 1)
                                dst = v[:, r, n // 3, :] if n % 3 == 2 else qk[:, r, n // 3, n % 3, :]
                                act.activation(dst, ps[:, g % 8, :], ACT.Copy).then_inc(taken, 1)

                    @block.vector
                    def _(dve):
                        step = Chain(dve, dstep)
                        for n in range(CB):
                            if n % 3 == 2:
                                continue
                            for r in range(R):
                                dve.wait_ge(taken, n * R + r + 1)
                                x = qk[:, r, n // 3, n % 3, :].rearrange("p (h d) -> p h d", h=H)
                                xa, xb = x[:, :, 0:ROPE_HALF], x[:, :, ROPE_HALF:2 * ROPE_HALF]
                                rows = lambda t_: t_[:, r:r + 1, :].to_broadcast([P, H, ROPE_HALF])
                                step(nc.vector.tensor_tensor(t1[:, 0, :, :], xa, rows(cos), ALU.mult))
                                step(nc.vector.tensor_tensor(t1[:, 1, :, :], xb, rows(sin), ALU.mult))
                                step(nc.vector.tensor_tensor(t2[:, 0, :, :], xb, rows(cos), ALU.mult))
                                step(nc.vector.tensor_tensor(t2[:, 1, :, :], xa, rows(sin), ALU.mult))
                                step(nc.vector.tensor_tensor(xa, t1[:, 0, :, :], t1[:, 1, :, :], ALU.subtract))
                                step(nc.vector.tensor_tensor(xb, t2[:, 0, :, :], t2[:, 1, :, :], ALU.add))
            transpose_stage(nc, k, "att_turn", [([qk[:, r, g, w, q * P:(q + 1) * P] for q in range(4)], kqt[:, g, w, :, r, :])
                                                for g in range(G) for w in range(2) for r in range(R)])
        with Stage(nc, "att_core") as st:
            KEYS = T + 2 * P
            m0, m12 = st.sb("m0", [P, R, R, P]), st.sb("m12", [P, 2, P])
            apart = st.sb("apart", [P, P], I32)
            s_ = st.sb("s", [P, 2, KEYS])
            pr = st.sb("pr", [P, 2, KEYS])
            pt = st.sb("pt", [P, 2, 6, P])
            top, ntop, l, rl = (st.sb(n, [P, 2]) for n in ("top", "ntop", "l", "rl"))
            psc = st.ps("psc", [P, 2, 2, BANK])
            pst = st.ps("pst", [P, 2, BANK])
            pso = st.ps("pso", [P, 2, BANK])
            names = ("pool_step", "apart_done", "bits_done", "masks_done", "s_made", "s_taken", "max_done", "exp_done", "inv_done", "norm_done",
                     "t_made", "t_taken", "o_made", "o_taken", "dve_step")
            s = {n: st.sem(n) for n in names}
            ITEMS = R * H
            SCALE = ATT_HD ** -0.5
            with nc.Block() as block:
                @block.gpsimd
                def _(pool):
                    step = Chain(pool, s["pool_step"])
                    nc.gpsimd.iota(apart[:, :], pattern=[[-1, P]], base=T, channel_multiplier=1).then_inc(s["apart_done"], 1)
                    step(nc.gpsimd.memset(m0[:, :, :, :], 0.0))
                    for base, sign in ((0, 1), (P, -1)):
                        step(nc.gpsimd.affine_select(out=m0[:, :, :, :], in_=m0[:, :, :, :], compare_op=ALU.is_ge, fill=NEG, base=base,
                                                     pattern=[[sign, R], [-sign, R], [-4 * sign, P]], channel_multiplier=4 * sign))
                    step(nc.gpsimd.memset(m12[:, 0, :], 0.0))
                    pool.wait_ge(s["bits_done"], 1)
                    for w in range(2):
                        step(nc.gpsimd.affine_select(out=m12[:, w, :], in_=m12[:, w, :], compare_op=ALU.is_ge, fill=NEG, base=0,
                                                     pattern=[[-1, P]], channel_multiplier=1))
                    pool.sem_inc(s["masks_done"], 1)
                    for n in range(ITEMS):
                        b = n % 2
                        pool.wait_ge(s["inv_done"], n + 1)
                        nc.gpsimd.tensor_scalar(pr[:, b, :], pr[:, b, :], rl[:, b:b + 1], None, ALU.mult).then_inc(s["norm_done"], 1)

                @block.tensor
                def _(pe):
                    def scores(n):
                        r, h, b = n // H, n % H, n % 2
                        f, q = slice(64 * (h % 2), 64 * (h % 2) + 64), h // 2
                        if n >= 2:
                            pe.wait_ge(s["s_taken"], n - 1)
                        nc.tensor.matmul(psc[:, b, 0, :], kqt[f, 0, 0, q, r, :], kqt[f, 0, 1, q, :, :], start=True, stop=True)
                        for g in (1, 2):
                            last = nc.tensor.matmul(psc[:, b, 1, (g - 1) * P:g * P], kqt[f, g, 0, q, r, :], kqt[f, g, 1, q, r, :], start=True, stop=True)
                        last.then_inc(s["s_made"], 1)

                    scores(0)
                    for n in range(ITEMS):
                        r, h, b = n // H, n % H, n % 2
                        f = slice(64 * (h % 2), 64 * (h % 2) + 64)
                        if n + 1 < ITEMS:
                            scores(n + 1)
                        pe.wait_ge(s["norm_done"], n + 1)
                        if n:
                            pe.wait_ge(s["t_taken"], n)
                        for m in range(6):
                            last = nc.tensor.transpose(pst[:, m // 4, (m % 4) * P:(m % 4 + 1) * P], pr[:, b, m * P:(m + 1) * P], k.ident[:, :])
                        last.then_inc(s["t_made"], 1)
                        pe.wait_ge(s["t_taken"], n + 1)
                        if n >= 4 and n % 2 == 0:
                            pe.wait_ge(s["o_taken"], n // 2 - 1)
                        accumulate(nc, pso[f, (n // 2) % 2, 0:P],
                                   [(v[:, (m if m < 4 else r), max(0, m - 3), h * ATT_HD:(h + 1) * ATT_HD], pt[:, b, m, :]) for m in range(6)]
                                   ).then_inc(s["o_made"], 1)

                @block.scalar
                def _(act):
                    for n in range(ITEMS):
                        b = n % 2
                        act.wait_ge(s["max_done"], n + 1)
                        if n >= 2:
                            act.wait_ge(s["t_made"], n - 1)
                        act.activation(pr[:, b, :], s_[:, b, :], ACT.Exp, bias=ntop[:, b:b + 1], scale=SCALE, accum_out=l[:, b:b + 1]).then_inc(s["exp_done"], 1)
                        act.wait_ge(s["t_made"], n + 1)
                        if n >= 2:
                            act.wait_ge(s["o_made"], n - 1)
                        act.activation(pt[:, b, 0:4, :], pst[:, 0, :].rearrange("p (a t) -> p a t", a=4), ACT.Copy)
                        act.activation(pt[:, b, 4:6, :], pst[:, 1, 0:2 * P].rearrange("p (a t) -> p a t", a=2), ACT.Copy).then_inc(s["t_taken"], 1)

                @block.vector
                def _(dve):
                    step = Chain(dve, s["dve_step"])
                    dve.wait_ge(s["apart_done"], 1)
                    step(nc.vector.tensor_scalar(apart[:, :], apart[:, :], 3, None, ALU.bitwise_and))
                    step(nc.vector.tensor_scalar(m12[:, 1, :], apart[:, :], 0.0, None, ALU.is_equal))
                    step(nc.vector.tensor_scalar(m12[:, 1, :], m12[:, 1, :], -1.0, -NEG, ALU.add, ALU.mult))
                    dve.sem_inc(s["bits_done"], 1)
                    dve.wait_ge(s["masks_done"], 1)

                    def first(n):
                        r, h, b = n // H, n % H, n % 2
                        dve.wait_ge(s["s_made"], n + 1)
                        if n >= 2:
                            dve.wait_ge(s["exp_done"], n - 1)
                        step(nc.vector.tensor_tensor(s_[:, b, 0:T], psc[:, b, 0, :], m0[:, r, :, :].rearrange("p a b -> p (a b)"), ALU.add))
                        nc.vector.tensor_tensor(s_[:, b, T:KEYS], psc[:, b, 1, 0:2 * P], m12[:, :, :].rearrange("p a b -> p (a b)"), ALU.add).then_inc(s["s_taken"], 1)
                        dve.wait_ge(s["s_taken"], n + 1)
                        step(nc.vector.tensor_reduce(top[:, b:b + 1], s_[:, b, :], AX.X, ALU.max))
                        nc.vector.tensor_scalar(ntop[:, b:b + 1], top[:, b:b + 1], -SCALE, None, ALU.mult).then_inc(s["max_done"], 1)

                    first(0)
                    for n in range(ITEMS):
                        r, h, b = n // H, n % H, n % 2
                        if n + 1 < ITEMS:
                            first(n + 1)
                        dve.wait_ge(s["exp_done"], n + 1)
                        if n >= 2:
                            dve.wait_ge(s["norm_done"], n - 1)
                        nc.vector.reciprocal(rl[:, b:b + 1], l[:, b:b + 1]).then_inc(s["inv_done"], 1)
                        if n % 2:
                            dve.wait_ge(s["o_made"], n + 1)
                            nc.vector.tensor_copy(ot[:, h // 2, r:T:R], pso[:, (n // 2) % 2, 0:P]).then_inc(s["o_taken"], 1)
        project_norm_stage(nc, k, "att_norm", ot, 4, a["attn_w_o_2"][0], None, ln_g, ln_b)


MOE_GROUPS, MOE_PER, MOE_EXPERTS, MOE_HIDDEN = 4, 8, 32, 512
SLOTS = 64
ASSIGN = 2 * T
MAX_BLOCKS = 48
ROUNDS = T // SLOTS


def moe_stages(nc, k, a, l):
    E, HID, HK = MOE_EXPERTS, MOE_HIDDEN, MOE_HIDDEN // P
    x_rows = nc.dram_tensor(f"x_rows{l}", (ASSIGN + 2 * SLOTS, D), F32).ap()
    y_rows = nc.dram_tensor(f"y_rows{l}", (MAX_BLOCKS * SLOTS, D), F32).ap()
    with Stage(nc, f"moe{l}") as outer:
        gates = outer.sb("gates", [P, TT, 2])
        xi, yi = outer.sb("xi", [P, TT, 2], U32), outer.sb("yi", [P, TT, 2], U32)
        info = outer.sb("info", [P, 2 * MAX_BLOCKS + 1], I32)
        with Stage(nc, f"route{l}") as st:
            wr = st.sb("wr", [P, DK, MOE_GROUPS + E])
            br = st.sb("br", [P, MOE_GROUPS + E])
            io = st.sb("io", [P, MAX_BLOCKS])
            iom = st.sb("iom", [P, MOE_PER])
            zero = st.sb("zero", [P, D])
            lg = st.sb("lg", [P, TT, MOE_GROUPS + E])
            mx, mi, tmp, m2 = (st.sb(n, [P, TT]) for n in ("mx", "mi", "tmp", "m2"))
            ohg, eg = st.sb("ohg", [P, TT, MOE_GROUPS]), st.sb("eg", [P, TT, MOE_GROUPS])
            es, e2, cand = (st.sb(n, [P, TT, MOE_PER]) for n in ("es", "e2", "cand"))
            oh = [st.sb(f"oh{j}", [P, TT, MOE_PER]) for j in range(2)]
            big = st.sb("big", [P, TT, MOE_GROUPS, MOE_PER])
            mj = [st.sb(f"mj{j}", [P, TT, E]) for j in range(2)]
            m = st.sb("m", [P, TT, E])
            cnt, nblk, cend, bend, start, bstart, off = (st.sb(n, [P, E]) for n in ("cnt", "nblk", "cend", "bend", "start", "bstart", "off"))
            cmp_ = st.sb("cmp", [P, E, ROUNDS])
            pos = st.sb("pos", [P, TT, E])
            rowf = st.sb("rowf", [P, TT])
            wide = st.sb("wide", [P, MAX_BLOCKS, E])
            be, xs = st.sb("be", [P, MAX_BLOCKS]), st.sb("xs", [P, MAX_BLOCKS])
            ew = st.sb("ew", [P, TT])
            gw = st.sb("gw", [P, TT])
            plg, prk, pct = st.ps("plg", [P, TT, MOE_GROUPS + E]), st.ps("prk", [P, TT, E]), st.ps("pct", [P, E])
            names = ("loaded", "logits_made", "iota_done", "dve_step", "exp_asked", "exp_done", "m_done", "counted", "rows_done", "zero_in", "zeroed", "sent")
            s = {n: st.sem(n) for n in names}
            with nc.Block() as block:
                @block.sync
                def _(sp):
                    sp.dma_start(wr[:, :, 0:MOE_GROUPS], a["moe_w_router_group_2"][l].rearrange("(k p) n -> p k n", p=P)).then_inc(s["loaded"], 16)
                    sp.dma_start(wr[:, :, MOE_GROUPS:], a["moe_w_router_expert_2"][l].rearrange("(k p) n -> p k n", p=P)).then_inc(s["loaded"], 16)
                    sp.dma_start(br[:, 0:MOE_GROUPS], row_broadcast(a["moe_b_router_group_2"][l])).then_inc(s["loaded"], 16)
                    sp.dma_start(br[:, MOE_GROUPS:], row_broadcast(a["moe_b_router_expert_2"][l])).then_inc(s["loaded"], 16)
                    sp.wait_ge(s["zeroed"], 1)
                    sp.dma_start(x_rows[ASSIGN:ASSIGN + 2 * SLOTS, :], zero[:, :]).then_inc(s["zero_in"], 16)
                    n_fill = 0
                    for r in range(ASSIGN, MAX_BLOCKS * SLOTS, P):
                        sp.dma_start(y_rows[r:r + P, :], zero[:, :]).then_inc(s["zero_in"], 16)
                        n_fill += 1
                    sp.wait_ge(s["loaded"], 64)
                    sp.wait_ge(s["zero_in"], 16 + 16 * n_fill)

                @block.tensor
                def _(pe):
                    pe.wait_ge(s["loaded"], 64)
                    for tt in range(TT):
                        last = accumulate(nc, plg[:, tt, :], [(k.ut[:, kk, 1 + tt * P:1 + (tt + 1) * P], wr[:, kk, :]) for kk in range(DK)])
                    last.then_inc(s["logits_made"], 1)
                    pe.wait_ge(s["m_done"], 1)
                    for tt in range(TT):
                        accumulate(nc, prk[:, tt, :], [(k.causal[:, 0, :], m[:, tt, :])] + [(k.ones[:, :], m[:, q, :]) for q in range(tt)])
                    accumulate(nc, pct[:, :], [(k.ones[:, :], m[:, q, :]) for q in range(TT)]).then_inc(s["counted"], 1)

                @block.scalar
                def _(act):
                    act.wait_ge(s["exp_asked"], 1)
                    act.activation(eg[:, :, :], eg[:, :, :], ACT.Exp).then_inc(s["exp_done"], 1)
                    act.wait_ge(s["exp_asked"], 2)
                    act.activation(ew[:, :], ew[:, :], ACT.Exp).then_inc(s["exp_done"], 1)

                @block.gpsimd
                def _(pool):
                    nc.gpsimd.memset(zero[:, :], 0.0).then_inc(s["zeroed"], 1)
                    nc.gpsimd.iota(io[:, :], pattern=[[1, MAX_BLOCKS]], base=0, channel_multiplier=0, allow_small_or_imprecise_dtypes=True).then_inc(s["iota_done"], 1)
                    nc.gpsimd.iota(iom[:, :], pattern=[[1, MOE_PER]], base=-64, channel_multiplier=0, allow_small_or_imprecise_dtypes=True).then_inc(s["iota_done"], 1)
                    pool.wait_ge(s["rows_done"], 1)
                    for tt in range(TT):
                        for j in range(2):
                            nc.gpsimd.indirect_dma_start(out=x_rows[:, :], out_offset=bass.IndirectOffsetOnAxis(ap=xi[:, tt, j:j + 1], axis=0),
                                                         in_=k.x[:, tt, :], in_offset=None).then_inc(s["sent"], 16)
                    pool.wait_ge(s["sent"], 16 * 2 * TT)

                @block.vector
                def _(dve):
                    step = Chain(dve, s["dve_step"])
                    V = nc.vector
                    dve.wait_ge(s["loaded"], 64)
                    dve.wait_ge(s["logits_made"], 1)
                    dve.wait_ge(s["iota_done"], 2)
                    bt = lambda ap, n: ap.unsqueeze(2).to_broadcast([P, TT, n])
                    row = lambda ap, n: ap.rearrange("p (a n) -> p a n", a=1).to_broadcast([P, TT, n])
                    step(V.tensor_tensor(lg[:, :, :], plg[:, :, :], row(br[:, :], MOE_GROUPS + E), ALU.add))

                    def arg_max(vals, n, onehot, scratch, best):
                        step(V.tensor_reduce(best, vals, AX.X, ALU.max))
                        step(V.tensor_tensor(scratch, vals, bt(best, n), ALU.is_equal))
                        step(V.tensor_tensor(scratch, scratch, row(iom[:, 0:n], n), ALU.mult))
                        step(V.tensor_reduce(mi[:, :], scratch, AX.X, ALU.min))
                        step(V.tensor_tensor(onehot, row(iom[:, 0:n], n), bt(mi[:, :], n), ALU.is_equal))

                    gl = lg[:, :, 0:MOE_GROUPS]
                    arg_max(gl, MOE_GROUPS, ohg[:, :, :], eg[:, :, :], mx[:, :])
                    step(V.tensor_tensor(eg[:, :, :], gl, bt(mx[:, :], MOE_GROUPS), ALU.subtract))
                    dve.sem_inc(s["exp_asked"], 1)
                    le = lg[:, :, MOE_GROUPS:].rearrange("p t (g e) -> p t g e", g=MOE_GROUPS)
                    for tt in range(TT):
                        step(V.tensor_tensor(big[:, tt, :, :], le[:, tt, :, :], ohg[:, tt, :].unsqueeze(2).to_broadcast([P, MOE_GROUPS, MOE_PER]), ALU.mult))
                        step(V.tensor_reduce(es[:, tt, :], big[:, tt, :, :].rearrange("p g e -> p e g"), AX.X, ALU.add))
                    arg_max(es[:, :, :], MOE_PER, oh[0][:, :, :], cand[:, :, :], mx[:, :])
                    step(V.scalar_tensor_tensor(e2[:, :, :], oh[0][:, :, :], NEG, es[:, :, :], ALU.mult, ALU.add))
                    arg_max(e2[:, :, :], MOE_PER, oh[1][:, :, :], cand[:, :, :], m2[:, :])
                    step(V.tensor_tensor(ew[:, :], m2[:, :], mx[:, :], ALU.subtract))
                    dve.sem_inc(s["exp_asked"], 1)
                    for j in range(2):
                        for tt in range(TT):
                            step(V.tensor_tensor(mj[j][:, tt, :].rearrange("p (g e) -> p g e", g=MOE_GROUPS),
                                                 ohg[:, tt, :].unsqueeze(2).to_broadcast([P, MOE_GROUPS, MOE_PER]),
                                                 oh[j][:, tt:tt + 1, :].to_broadcast([P, MOE_GROUPS, MOE_PER]), ALU.mult))
                    V.tensor_tensor(m[:, :, :], mj[0][:, :, :], mj[1][:, :, :], ALU.add).then_inc(s["m_done"], 1)
                    dve.wait_ge(s["exp_done"], 2)
                    step(V.tensor_reduce(gw[:, :], eg[:, :, :], AX.X, ALU.add))
                    step(V.tensor_scalar(tmp[:, :], ew[:, :], 1.0, None, ALU.add))
                    step(V.tensor_tensor(gw[:, :], gw[:, :], tmp[:, :], ALU.mult))
                    step(V.reciprocal(gates[:, :, 0], gw[:, :]))
                    step(V.tensor_tensor(gates[:, :, 1], gates[:, :, 0], ew[:, :], ALU.mult))
                    dve.wait_ge(s["counted"], 1)
                    step(V.tensor_copy(cnt[:, :], pct[:, :]))
                    step(V.tensor_scalar(be[:, 0:ROUNDS], io[:, 0:ROUNDS], float(SLOTS), None, ALU.mult))
                    step(V.tensor_tensor(cmp_[:, :, :], cnt[:, :].unsqueeze(2).to_broadcast([P, E, ROUNDS]),
                                         be[:, 0:ROUNDS].rearrange("p (a r) -> p a r", a=1).to_broadcast([P, E, ROUNDS]), ALU.is_gt))
                    step(V.tensor_reduce(nblk[:, :], cmp_[:, :, :], AX.X, ALU.add))
                    step(V.tensor_tensor_scan(cend[:, :], k.ones[:, 0:E], cnt[:, :], 0.0, ALU.mult, ALU.add))
                    step(V.tensor_tensor_scan(bend[:, :], k.ones[:, 0:E], nblk[:, :], 0.0, ALU.mult, ALU.add))
                    step(V.tensor_tensor(start[:, :], cend[:, :], cnt[:, :], ALU.subtract))
                    step(V.tensor_tensor(bstart[:, :], bend[:, :], nblk[:, :], ALU.subtract))
                    step(V.tensor_scalar(bstart[:, :], bstart[:, :], float(SLOTS), None, ALU.mult))
                    for base, dst in ((start, xi), (bstart, yi)):
                        step(V.tensor_tensor(pos[:, :, :], prk[:, :, :], row(base[:, :], E), ALU.add))
                        for j in range(2):
                            step(V.tensor_tensor(big[:, :, :, :].rearrange("p t g e -> p t (g e)"), pos[:, :, :], mj[j][:, :, :], ALU.mult))
                            step(V.tensor_reduce(rowf[:, :], big[:, :, :, :].rearrange("p t g e -> p t (g e)"), AX.X, ALU.add))
                            step(V.tensor_copy(dst[:, :, j], rowf[:, :]))
                        if dst is xi:
                            dve.sem_inc(s["rows_done"], 1)
                    B = MAX_BLOCKS
                    per_b = lambda ap: ap.rearrange("p (a e) -> p a e", a=1).to_broadcast([P, B, E])
                    per_e = lambda ap: ap.unsqueeze(2).to_broadcast([P, B, E])
                    step(V.tensor_tensor(wide[:, :, :], per_b(bend[:, :]), per_e(io[:, :]), ALU.is_le))
                    step(V.tensor_reduce(be[:, :], wide[:, :, :], AX.X, ALU.add))
                    step(V.tensor_scalar(be[:, :], be[:, :], float(E - 1), None, ALU.min))
                    step(V.tensor_copy(info[:, 0:B], be[:, :]))
                    step(V.tensor_tensor(off[:, :], start[:, :], bstart[:, :], ALU.subtract))
                    step(V.tensor_tensor(wide[:, :, :], per_b(io[:, 0:E]), per_e(be[:, :]), ALU.is_equal))
                    step(V.tensor_tensor(wide[:, :, :], wide[:, :, :], per_b(off[:, :]), ALU.mult))
                    step(V.tensor_reduce(xs[:, :], wide[:, :, :], AX.X, ALU.add))
                    step(V.scalar_tensor_tensor(xs[:, :], io[:, :], float(SLOTS), xs[:, :], ALU.mult, ALU.add))
                    step(V.tensor_scalar(xs[:, :], xs[:, :], float(ASSIGN + SLOTS), 0.0, ALU.min, ALU.max))
                    step(V.tensor_copy(info[:, B:2 * B], xs[:, :]))
                    step(V.tensor_tensor(be[:, 0:B // 2], io[:, 0:B:2], bend[:, E - 1:E].to_broadcast([P, B // 2]), ALU.is_lt))
                    step(V.tensor_reduce(rowf[:, 0:1], be[:, 0:B // 2], AX.X, ALU.add))
                    step(V.tensor_scalar(rowf[:, 0:1], rowf[:, 0:1], -1.0, None, ALU.add))
                    step(V.tensor_copy(info[:, 2 * B:2 * B + 1], rowf[:, 0:1]))

        with Stage(nc, f"experts{l}") as st:
            wg, wd = st.sb("wg", [P, 2, 2, DK, HID]), st.sb("wd", [P, 2, HK, D])
            HALF = D // 2
            MQ = HALF // P
            xg, yb = st.sb("xg", [P, 2, HALF]), st.sb("yb", [P, 2, HALF])
            xt, yt = st.sb("xt", [P, 2, MQ, 2, SLOTS]), st.sb("yt", [P, 2, MQ, 2, SLOTS])
            hs, h = st.sb("hs", [P, 2, HK * SLOTS]), st.sb("h", [P, 2, HK, SLOTS])
            px, pg, pd, py = (st.ps("px", [P, MQ, P]), st.ps("pg", [P, 2, 2, HK, SLOTS]), st.ps("pd", [P, MQ, 2, SLOTS]),
                              st.ps("py", [P, MQ, P]))
            x_in, gu_in, d_in, stored = ([st.sem(f"{n}{b}") for b in range(2)] for n in ("x_in", "gu_in", "d_in", "stored"))
            names = ("xt_made", "xt_taken", "gu_made", "silu_done", "h_done", "d_made", "d_taken", "y_made", "y_taken")
            s = {n: st.sem(n) for n in names}
            w_gate, w_up = (a[f"moe_{n}_2"][l].rearrange("e (k p) n -> p e k n", p=P) for n in ("w_gate", "w_up"))
            w_down = a["moe_w_down_2"][l].rearrange("e (k p) n -> p e k n", p=P)
            B = MAX_BLOCKS

            def pairs_after_first(eng):
                return eng.value_load(info[0:1, 2 * B:2 * B + 1], min_val=ASSIGN // SLOTS // 2 - 1, max_val=B // 2 - 1)

            with nc.Block() as block:
                @block.sync
                def _(sp):
                    more = pairs_after_first(sp)

                    def load(i, b, first=False):
                        e = sp.value_load(info[0:1, bass.ds(i, 1)], min_val=0, max_val=E - 1)
                        r0 = sp.value_load(info[0:1, bass.ds(i + B, 1)], min_val=0, max_val=ASSIGN + SLOTS)
                        if not first:
                            sp.wait_ge(s["xt_made"], i - 1)
                        for half in range(2):
                            sp.dma_start(xg[half * SLOTS:(half + 1) * SLOTS, b, :],
                                         x_rows[bass.ds(r0, SLOTS), half * HALF:(half + 1) * HALF]).then_inc(x_in[b], 16)
                        if not first:
                            sp.wait_ge(s["gu_made"], i - 1)
                        for side, w in enumerate((w_gate, w_up)):
                            sp.dma_start(wg[:, b, side, :, :], w[:, bass.ds(e, 1), :, :]).then_inc(gu_in[b], 16)
                        if not first:
                            sp.wait_ge(s["d_made"], i - 1)
                        sp.dma_start(wd[:, b, :, :], w_down[:, bass.ds(e, 1), :, :]).then_inc(d_in[b], 16)

                    load(0, 0, True)
                    load(1, 1, True)
                    with sp.Fori(1, more + 1) as it:
                        for b in range(2):
                            load(2 * it + b, b)

                @block.tensor
                def _(pe):
                    more = pairs_after_first(pe)

                    def y_turn(n, b, first=False):
                        pe.wait_ge(s["d_taken"], n + 1)
                        if not first:
                            pe.wait_ge(s["y_taken"], n)
                        for m in range(MQ):
                            last = nc.tensor.transpose(py[:, m, :], yt[:, b, m, :, :].rearrange("p a s -> p (a s)"), k.ident[:, :])
                        last.then_inc(s["y_made"], 1)

                    def one(n, b, it, first=False):
                        pe.wait_ge(x_in[b], 32 * it + 32)
                        if not first:
                            pe.wait_ge(s["xt_taken"], n)
                        for m in range(MQ):
                            last = nc.tensor.transpose(px[:, m, :], xg[:, b, m * P:(m + 1) * P], k.ident[:, :])
                        last.then_inc(s["xt_made"], 1)
                        pe.wait_ge(gu_in[b], 32 * it + 32)
                        pe.wait_ge(s["xt_taken"], n + 1)
                        for side in range(2):
                            for q in range(HK):
                                last = accumulate(nc, pg[:, b, side, q, :], [(wg[:, b, side, kk, q * P:(q + 1) * P], xt[:, b, kk % MQ, kk // MQ, :]) for kk in range(DK)])
                        last.then_inc(s["gu_made"], 1)
                        if not first:
                            y_turn(n - 1, 1 - b, first == 1)
                        pe.wait_ge(d_in[b], 16 * it + 16)
                        pe.wait_ge(s["h_done"], n + 1)
                        for d in range(DK):
                            last = accumulate(nc, pd[:, d % MQ, d // MQ, :], [(wd[:, b, q, d * P:(d + 1) * P], h[:, b, q, :]) for q in range(HK)])
                        last.then_inc(s["d_made"], 1)

                    one(0, 0, 0, True)
                    pe.wait_ge(x_in[1], 32)
                    pe.wait_ge(s["xt_taken"], 1)
                    for m in range(MQ):
                        last = nc.tensor.transpose(px[:, m, :], xg[:, 1, m * P:(m + 1) * P], k.ident[:, :])
                    last.then_inc(s["xt_made"], 1)
                    pe.wait_ge(gu_in[1], 32)
                    pe.wait_ge(s["xt_taken"], 2)
                    for side in range(2):
                        for q in range(HK):
                            last = accumulate(nc, pg[:, 1, side, q, :], [(wg[:, 1, side, kk, q * P:(q + 1) * P], xt[:, 1, kk % MQ, kk // MQ, :]) for kk in range(DK)])
                    last.then_inc(s["gu_made"], 1)
                    y_turn(0, 0, True)
                    pe.wait_ge(d_in[1], 16)
                    pe.wait_ge(s["h_done"], 2)
                    for d in range(DK):
                        last = accumulate(nc, pd[:, d % MQ, d // MQ, :], [(wd[:, 1, q, d * P:(d + 1) * P], h[:, 1, q, :]) for q in range(HK)])
                    last.then_inc(s["d_made"], 1)
                    with pe.Fori(1, more + 1) as it:
                        for b in range(2):
                            one(2 * it + b, b, it)
                    y_turn(2 * more + 1, 1)

                @block.scalar
                def _(act):
                    more = pairs_after_first(act)

                    def one(n, b, first=False):
                        act.wait_ge(s["gu_made"], n + 1)
                        if not first:
                            act.wait_ge(s["h_done"], n - 1)
                        act.activation(hs[:, b, :], pg[:, b, 0, :, :].rearrange("p a b -> p (a b)"), ACT.Silu).then_inc(s["silu_done"], 1)
                        act.wait_ge(s["d_made"], n + 1)
                        if not first:
                            act.wait_ge(s["y_made"], n - 1)
                        act.activation(yt[:, b, :, :, :], pd[:, :, :, :], ACT.Copy).then_inc(s["d_taken"], 1)

                    one(0, 0, True)
                    one(1, 1, True)
                    with act.Fori(1, more + 1) as it:
                        for b in range(2):
                            one(2 * it + b, b)

                @block.vector
                def _(dve):
                    more = pairs_after_first(dve)

                    def y_take(n, b, it, first=False):
                        dve.wait_ge(s["y_made"], n + 1)
                        if not first:
                            dve.wait_ge(stored[b], 32 * it)
                        nc.vector.tensor_copy(yb[:, b, :], py[:, :, :].rearrange("p a b -> p (a b)")).then_inc(s["y_taken"], 1)

                    def one(n, b):
                        dve.wait_ge(s["xt_made"], n + 1)
                        nc.vector.tensor_copy(xt[:, b, :, :, :].rearrange("p m a s -> p m (a s)"), px[:, :, :]).then_inc(s["xt_taken"], 1)
                        dve.wait_ge(s["silu_done"], n + 1)
                        nc.vector.tensor_tensor(h[:, b, :, :].rearrange("p a b -> p (a b)"), hs[:, b, :],
                                                pg[:, b, 1, :, :].rearrange("p a b -> p (a b)"), ALU.mult).then_inc(s["h_done"], 1)

                    one(0, 0)
                    one(1, 1)
                    y_take(0, 0, 0, True)
                    one(2, 0)
                    y_take(1, 1, 0, True)
                    one(3, 1)
                    y_take(2, 0, 1)
                    with dve.Fori(2, more + 1) as it:
                        one(2 * it, 0)
                        y_take(2 * it - 1, 1, it - 1)
                        one(2 * it + 1, 1)
                        y_take(2 * it, 0, it)
                    y_take(2 * more + 1, 1, more)

                @block.gpsimd
                def _(pool):
                    more = pairs_after_first(pool)
                    with pool.Fori(0, more + 1) as it:
                        for b in range(2):
                            n = 2 * it + b
                            pool.wait_ge(s["y_taken"], n + 1)
                            for half in range(2):
                                pool.dma_start(y_rows[bass.ds(n * SLOTS, SLOTS), half * HALF:(half + 1) * HALF],
                                               yb[half * SLOTS:(half + 1) * SLOTS, b, :]).then_inc(stored[b], 16)
                    for b in range(2):
                        pool.wait_ge(stored[b], 32 * more + 32)

        with Stage(nc, f"merge{l}") as st:
            g, b = st.sb("g", [P, D]), st.sb("b", [P, D])
            norm = Norm(nc, k, st, None, g, b)
            yg = st.sb("yg", [P, TT, 2, D])
            y = st.sb("y", [P, D])
            rows_in, dstep = st.sem("rows_in"), st.sem("dve_step")
            got = [st.sem(f"got{tt}") for tt in range(TT)]
            with nc.Block() as block:
                @block.gpsimd
                def _(pool):
                    for tt in range(TT):
                        for j in range(2):
                            nc.gpsimd.indirect_dma_start(out=yg[:, tt, j, :], out_offset=None, in_=y_rows[:, :],
                                                         in_offset=bass.IndirectOffsetOnAxis(ap=yi[:, tt, j:j + 1], axis=0)).then_inc(got[tt], 16)

                @block.scalar
                def _(act):
                    act.dma_start(g[:, :], row_broadcast(a["ln_g_2"][l, 1])).then_inc(rows_in, 16)
                    act.dma_start(b[:, :], row_broadcast(a["ln_b_2"][l, 1])).then_inc(rows_in, 16)
                    act.wait_ge(rows_in, 32)
                    norm.square_root(act)

                @block.vector
                def _(dve):
                    step = Chain(dve, dstep)
                    dve.wait_ge(rows_in, 32)
                    for tt in range(TT):
                        dve.wait_ge(got[tt], 32)
                        step(nc.vector.tensor_scalar(y[:, :], yg[:, tt, 0, :], gates[:, tt, 0:1], None, ALU.mult))
                        step(nc.vector.scalar_tensor_tensor(y[:, :], yg[:, tt, 1, :], gates[:, tt, 1:2], y[:, :], ALU.mult, ALU.add))
                        norm.sums(step, tt, [y[:, half * BANK:(half + 1) * BANK] for half in range(2)])
                    norm.finish(dve, step)


def program(nc, a, out):
    ga_dram = nc.dram_tensor("ga_rows", (LAYERS, 2, D), F32).ap()
    r8 = lambda v: v.rearrange("(t p) -> t p", p=P)
    with ExitStack() as stack:
        sb = lambda name, shape, dt=F32: stack.enter_context(nc.sbuf_tensor(name, shape, dt))
        k = Kept()
        k.x = sb("x_tok", [P, TT, D])
        k.ut = sb("ut", [P, DK, T + 1])
        k.ident, k.ones, k.per_head = sb("ident", [P, P]), sb("ones", [P, P]), sb("per_head", [P, P])
        k.causal, k.level = sb("causal", [P, 2, P]), sb("level", [P, 7, P])
        k.cola, k.colb, k.colc = sb("cola", [P, A_ROWS]), sb("colb", [P, CONV * QKV_TILES]), sb("colc", [P, 5 * SSD_TILES])
        k.modc = sb("modc", [P, LAYERS, 4, DK])
        table_a = [a["rwkv_mu"][0].rearrange("i (t p) -> (i t) p", p=P)] + [r8(a[n][0]) for n in ("rwkv_w0", "rwkv_a0", "rwkv_k_k", "rwkv_k_a")] \
            + [a["rwkv_r_k"][0].rearrange("(t a) n -> t (a n)", a=2), a["c"].rearrange("a (t p) -> (a t) p", p=P)]
        table_b = [a["gdn_conv"][0].rearrange("k (t p) -> (k t) p", p=P)]
        table_c = [a["ssd_conv_w_2"][0].rearrange("k (t p) -> (k t) p", p=P), r8(a["ssd_conv_b_2"][0])]
        constants_stage(nc, k, [table_a, table_b, table_c])
        load_x_stage(nc, k, a["x"][0])
        ada_stage(nc, k, a["ada_w"], a["ada_b"], ga_dram)
        mod = lambda l, part: k.modc[:, l, part, :]

        turn_stage(nc, k, "turn0", mod(0, 1), mod(0, 0))
        p = {n: a["rwkv_" + n][0] for n in ("w_rkv", "w1", "w2", "a1", "a2", "g1", "g2", "w_out")}
        rwkv_stages(nc, k, p, ga_dram[0, 0], a["ln_g"][0, 0], a["ln_b"][0, 0], a["rwkv_gn_g"][0], a["rwkv_gn_b"][0])
        turn_stage(nc, k, "turn1", mod(0, 3), mod(0, 2))
        ffn_stages(nc, k, 0, a["ffn_w_in"][0], a["ffn_w_out"][0], ga_dram[0, 1], a["ln_g"][0, 1], a["ln_b"][0, 1])
        turn_stage(nc, k, "turn2", mod(1, 1), mod(1, 0))
        gdn_stages(nc, k, a, ga_dram[1, 0], a["ln_g"][1, 0], a["ln_b"][1, 0])
        turn_stage(nc, k, "turn3", mod(1, 3), mod(1, 2))
        ffn_stages(nc, k, 1, a["ffn_w_in"][1], a["ffn_w_out"][1], ga_dram[1, 1], a["ln_g"][1, 1], a["ln_b"][1, 1])
        turn_stage(nc, k, "turn4")
        ssd_stages(nc, k, a, a["ln_g_2"][0, 0], a["ln_b_2"][0, 0])
        turn_stage(nc, k, "turn5")
        moe_stages(nc, k, a, 0)
        turn_stage(nc, k, "turn6")
        attention_stages(nc, k, a, a["ln_g_2"][1, 0], a["ln_b_2"][1, 0])
        turn_stage(nc, k, "turn7")
        moe_stages(nc, k, a, 1)
        store_x_stage(nc, k, out[0])


class Kept:
    pass


def load_x_stage(nc, k, x):
    with Stage(nc, "load_x") as st:
        done = st.sem("done")
        with nc.Block() as block:
            @block.sync
            def _(sp):
                sp.dma_start(k.x[:, :, :], x.rearrange("(t p) n -> p t n", p=P)).then_inc(done, 16)
                sp.wait_ge(done, 16)


def store_x_stage(nc, k, out):
    with Stage(nc, "store_x") as st:
        done = st.sem("done")
        with nc.Block() as block:
            @block.sync
            def _(sp):
                sp.dma_start(out.rearrange("(t p) n -> p t n", p=P), k.x[:, :, :]).then_inc(done, 16)
                sp.wait_ge(done, 16)


def kernel(**inputs):
    import numpy as _np
    import concourse.bacc as _bacc
    from concourse.bass_utils import run_bass_kernel_spmd as _run

    nc = _bacc.Bacc("TRN2", target_bir_lowering=False, num_devices=1)
    arrays, args = {}, {}
    for name, value in inputs.items():
        if name.startswith(("diff_", "swa_")):
            continue
        a = _np.ascontiguousarray(value)
        arrays[f"in_{name}"] = a
        args[name] = nc.dram_tensor(f"in_{name}", a.shape, mybir.dt.from_np(a.dtype), kind="ExternalInput").ap()
    out = nc.dram_tensor("out_x", (1, T, D), F32, kind="ExternalOutput").ap()
    program(nc, args, out)
    r = _run(nc, [arrays], core_ids=[0])
    return r.results[0]["out_x"]
```
